# Optimizing a Trainium2 kernel written in Bass

```python
import jax, jax.numpy as jnp
from jax import lax
import numpy as np

D_MODEL = 2048
BATCH = 1
SEQ = 256
DEPTH = 2

MIX_WIDTH = D_MODEL
N_GROUPS = 4
GROUP_WIDTH = MIX_WIDTH // N_GROUPS
POOL_WINDOWS = (2, 4, 8, 16)
POOL_GROUP = GROUP_WIDTH // len(POOL_WINDOWS)
SGU_HEADS = 4
SGU_HEAD_DIM = GROUP_WIDTH // SGU_HEADS
SGU_CHUNK = 128
FOX_HEADS = 4
FOX_HEAD_DIM = GROUP_WIDTH // FOX_HEADS
FOX_BLOCK = 128
RET_HEADS = 4
RET_V_DIM = GROUP_WIDTH // RET_HEADS
RET_QK_DIM = RET_V_DIM // 2
RET_CHUNK = 128
ROPE_BASE = 10000.0
D_FF = 4 * D_MODEL
EPS = 1e-6
NEG_BIG = -1e30
SPLIT_SIZES = (GROUP_WIDTH,
               GROUP_WIDTH, GROUP_WIDTH,
               GROUP_WIDTH, GROUP_WIDTH, GROUP_WIDTH, FOX_HEADS,
               RET_HEADS * RET_QK_DIM, RET_HEADS * RET_QK_DIM, GROUP_WIDTH, GROUP_WIDTH)
IN_COLS = 9 * GROUP_WIDTH + FOX_HEADS + 2 * RET_HEADS * RET_QK_DIM

kernel_name = 'hymba_style_pool_sgu_fox_retention_hybrid'

def split_columns(proj):
    pieces, start = [], 0
    for size in SPLIT_SIZES:
        pieces.append(proj[..., start:start + size])
        start += size
    return pieces

def rmsnorm(x, g):
    xf = x.astype(jnp.float32)
    y = xf * lax.rsqrt(jnp.mean(xf * xf, axis=-1, keepdims=True) + EPS)
    return (y * g.astype(jnp.float32)).astype(x.dtype)

def head_layernorm(x, g, n_heads, head_dim):
    B, S, _ = x.shape
    xf = x.astype(jnp.float32).reshape(B, S, n_heads, head_dim)
    mu = jnp.mean(xf, axis=-1, keepdims=True)
    var = jnp.mean(jnp.square(xf - mu), axis=-1, keepdims=True)
    y = (xf - mu) * lax.rsqrt(var + EPS) * g.astype(jnp.float32).reshape(n_heads, head_dim)
    return y.reshape(B, S, n_heads * head_dim).astype(x.dtype)

def pool_mixer(a, pool_w, pool_scale):
    B, S, _ = a.shape
    af = a.astype(jnp.float32)
    cs = jnp.cumsum(af, axis=1)
    outs = []
    for gi, w in enumerate(POOL_WINDOWS):
        lo, hi = gi * POOL_GROUP, (gi + 1) * POOL_GROUP
        c = cs[..., lo:hi]
        c_prev = jnp.pad(c[:, :S - w], ((0, 0), (w, 0), (0, 0)))
        cnt = jnp.minimum(jnp.arange(1, S + 1, dtype=jnp.float32), float(w))[None, :, None]
        outs.append((c - c_prev) / cnt - af[..., lo:hi])
    p = jnp.stack(outs, axis=2).astype(a.dtype)
    y = jnp.einsum('bsgc,gcd->bsgd', p, pool_w).reshape(B, S, GROUP_WIDTH)
    return y * pool_scale

def sgu_mixer(u, v, norm_g, w_s, b_s):
    B, S, _ = u.shape
    u = jax.nn.gelu(u)
    v = head_layernorm(jax.nn.gelu(v), norm_g, SGU_HEADS, SGU_HEAD_DIM)
    vc = v.reshape(B, S // SGU_CHUNK, SGU_CHUNK, SGU_HEADS, SGU_HEAD_DIM)
    mask = jnp.tril(jnp.ones((SGU_CHUNK, SGU_CHUNK), dtype=jnp.float32)).astype(w_s.dtype)
    z = jnp.einsum('hts,bcshd->bcthd', w_s * mask[None], vc)
    z = z + jnp.transpose(b_s)[None, None, :, :, None]
    return u * z.reshape(B, S, GROUP_WIDTH)

def fox_mixer(q, k, v, f_logit, b_f):
    B, S, _ = q.shape
    q = q.reshape(B, S, FOX_HEADS, FOX_HEAD_DIM).transpose(0, 2, 1, 3)
    k = k.reshape(B, S, FOX_HEADS, FOX_HEAD_DIM).transpose(0, 2, 1, 3)
    v = v.reshape(B, S, FOX_HEADS, FOX_HEAD_DIM).transpose(0, 2, 1, 3)
    log_f = jax.nn.log_sigmoid(f_logit.astype(jnp.float32) + b_f.astype(jnp.float32))
    c = jnp.cumsum(log_f, axis=1).transpose(0, 2, 1)
    scale = FOX_HEAD_DIM ** -0.5
    outs = []
    for i in range(S // FOX_BLOCK):
        start, end = i * FOX_BLOCK, (i + 1) * FOX_BLOCK
        qb = q[:, :, start:end]
        kb = k[:, :, :end]
        vb = v[:, :, :end]
        cq = c[:, :, start:end]
        ck = c[:, :, :end]
        s = jnp.einsum('bhqd,bhkd->bhqk', qb, kb).astype(jnp.float32) * scale
        s = s + (cq[..., :, None] - ck[..., None, :])
        qpos = start + jnp.arange(FOX_BLOCK)
        kpos = jnp.arange(end)
        s = jnp.where(kpos[None, :] <= qpos[:, None], s, NEG_BIG)
        p = jax.nn.softmax(s, axis=-1)
        outs.append(jnp.einsum('bhqk,bhkd->bhqd', p.astype(vb.dtype), vb))
    o = jnp.concatenate(outs, axis=2)
    return o.transpose(0, 2, 1, 3).reshape(B, S, GROUP_WIDTH)

def rotary(x, pos):
    half = x.shape[-1] // 2
    inv = jnp.exp(-(jnp.arange(half, dtype=jnp.float32) / half) * np.float32(np.log(ROPE_BASE)))
    ang = pos[:, None] * inv[None, :]
    cos = jnp.cos(ang)[None, :, None, :]
    sin = jnp.sin(ang)[None, :, None, :]
    x1, x2 = x[..., :half], x[..., half:]
    return jnp.concatenate([x1 * cos - x2 * sin, x1 * sin + x2 * cos], axis=-1)

def retention_mixer(q, k, v, g, norm_g):
    B, S, _ = q.shape
    L = RET_CHUNK
    nC = S // L
    pos = jnp.arange(S, dtype=jnp.float32)
    qf = rotary(q.astype(jnp.float32).reshape(B, S, RET_HEADS, RET_QK_DIM), pos)
    kf = rotary(k.astype(jnp.float32).reshape(B, S, RET_HEADS, RET_QK_DIM), pos) * (RET_QK_DIM ** -0.5)
    vf = v.astype(jnp.float32).reshape(B, S, RET_HEADS, RET_V_DIM)
    gamma = 1.0 - jnp.exp((-5.0 - jnp.arange(RET_HEADS, dtype=jnp.float32)) * np.float32(np.log(2.0)))
    log_gamma = jnp.log(gamma)
    l = jnp.arange(L, dtype=jnp.float32)
    diff = l[:, None] - l[None, :]
    decay = jnp.where(diff[None] >= 0, jnp.exp(jnp.maximum(diff, 0.0)[None] * log_gamma[:, None, None]), 0.0)
    qc = qf.reshape(B, nC, L, RET_HEADS, RET_QK_DIM)
    kc = kf.reshape(B, nC, L, RET_HEADS, RET_QK_DIM)
    vc = vf.reshape(B, nC, L, RET_HEADS, RET_V_DIM)
    s = jnp.einsum('bclhd,bcmhd->bchlm', qc, kc) * decay[None, None]
    y_intra = jnp.einsum('bchlm,bcmhe->bclhe', s, vc)
    xi = jnp.exp((l + 1.0)[:, None] * log_gamma[None, :])
    zeta = jnp.exp((L - 1.0 - l)[:, None] * log_gamma[None, :])
    chunk_decay = jnp.exp(L * log_gamma)

    def step(R, inp):
        qi, ki, vi = inp
        y = jnp.einsum('blhd,bhde->blhe', qi, R) * xi[None, :, :, None]
        R = R * chunk_decay[None, :, None, None] + jnp.einsum('blhd,blhe->bhde', ki * zeta[None, :, :, None], vi)
        return R, y

    R0 = jnp.zeros((B, RET_HEADS, RET_QK_DIM, RET_V_DIM), jnp.float32)
    xs = (jnp.moveaxis(qc, 1, 0), jnp.moveaxis(kc, 1, 0), jnp.moveaxis(vc, 1, 0))
    _, y_cross = lax.scan(step, R0, xs)
    y = (y_intra + jnp.moveaxis(y_cross, 0, 1)).reshape(B, S, GROUP_WIDTH)
    y = head_layernorm(y, norm_g, RET_HEADS, RET_V_DIM).astype(g.dtype)
    return jax.nn.silu(g) * y

def setup_inputs(seed: int = 0) -> dict:
    key = jax.random.key(seed)
    ks = jax.random.split(key, 16)
    f32 = jnp.float32

    def nrm(k, shape, s):
        return jax.random.normal(k, shape, f32) * s

    return {
        'x': jax.random.normal(ks[0], (BATCH, SEQ, D_MODEL), f32),
        'norm_mix_g': 1.0 + nrm(ks[1], (DEPTH, D_MODEL), 0.05),
        'w_in': nrm(ks[2], (DEPTH, D_MODEL, IN_COLS), D_MODEL ** -0.5),
        'fox_b_f': 2.0 + nrm(ks[3], (DEPTH, FOX_HEADS), 0.5),
        'pool_w': nrm(ks[4], (DEPTH, len(POOL_WINDOWS), POOL_GROUP, POOL_GROUP), POOL_GROUP ** -0.5),
        'pool_scale': 1.0 + nrm(ks[5], (DEPTH, GROUP_WIDTH), 0.1),
        'sgu_norm_g': 1.0 + nrm(ks[6], (DEPTH, GROUP_WIDTH), 0.05),
        'sgu_w_s': nrm(ks[7], (DEPTH, SGU_HEADS, SGU_CHUNK, SGU_CHUNK), SGU_CHUNK ** -0.5),
        'sgu_b': 1.0 + nrm(ks[8], (DEPTH, SGU_HEADS, SGU_CHUNK), 0.1),
        'ret_norm_g': 1.0 + nrm(ks[9], (DEPTH, GROUP_WIDTH), 0.05),
        'w_out': nrm(ks[10], (DEPTH, MIX_WIDTH, D_MODEL), MIX_WIDTH ** -0.5),
        'norm_mlp_g': 1.0 + nrm(ks[11], (DEPTH, D_MODEL), 0.05),
        'w_ff1': nrm(ks[12], (DEPTH, D_MODEL, D_FF), D_MODEL ** -0.5),
        'w_ff2': nrm(ks[13], (DEPTH, D_FF, D_MODEL), D_FF ** -0.5),
        'norm_final_g': 1.0 + nrm(ks[14], (D_MODEL,), 0.05),
    }

def reference(x, norm_mix_g, w_in, fox_b_f, pool_w, pool_scale, sgu_norm_g, sgu_w_s, sgu_b,
              ret_norm_g, w_out, norm_mlp_g, w_ff1, w_ff2, norm_final_g):
    h = x
    for layer in range(DEPTH):
        xn = rmsnorm(h, norm_mix_g[layer])
        proj = jnp.einsum('bsd,dc->bsc', xn, w_in[layer])
        (a_in, u_in, v_in, q_f, k_f, v_f, f_logit,
         q_r, k_r, v_r, g_r) = split_columns(proj)
        y_a = pool_mixer(a_in, pool_w[layer], pool_scale[layer])
        y_b = sgu_mixer(u_in, v_in, sgu_norm_g[layer], sgu_w_s[layer], sgu_b[layer])
        y_c = fox_mixer(q_f, k_f, v_f, f_logit, fox_b_f[layer])
        y_d = retention_mixer(q_r, k_r, v_r, g_r, ret_norm_g[layer])
        mix = jnp.concatenate([y_a, y_b, y_c, y_d], axis=-1)
        h = h + jnp.einsum('bsc,cd->bsd', mix, w_out[layer])
        hn = rmsnorm(h, norm_mlp_g[layer])
        ff = jnp.square(jax.nn.relu(jnp.einsum('bsd,df->bsf', hn, w_ff1[layer])))
        h = h + jnp.einsum('bsf,fd->bsd', ff, w_ff2[layer])
    return rmsnorm(h, norm_final_g)


_drawn_inputs = setup_inputs


def setup_inputs(seed=0):
    import zlib

    import numpy as np

    out = dict(_drawn_inputs(seed))
    spreads = {}
    factors = {'sgu_norm_g': 4.136, 'ret_norm_g': 3.312}
    for name, (base, spread) in spreads.items():
        noise = np.random.default_rng([zlib.crc32(name.encode()), seed]).standard_normal(out[name].shape)
        drawn = base * np.exp(spread * noise) if base else spread * noise
        out[name] = __import__('jax').numpy.asarray(drawn.astype(out[name].dtype))
    for name, factor in factors.items():
        out[name] = (out[name] * factor).astype(out[name].dtype)
    return out
```

```python
import concourse.bass as bass
from concourse import mybir
from contextlib import ExitStack
import numpy as np

D = 2048
S = 256
DEPTH = 2
DFF = 4 * D
GW = D // 4
P = 128
NT = S // P
KT = D // P
NH = 4
HD = GW // NH
RQK = HD // 2
WINDOWS = (2, 4, 8, 16)
EPS = 1e-6
NEG_BIG = -1e30
Q_SCALE = HD ** -0.5
CW = 512
FCOLS = NH
CHUNKS = 8
CK = KT // CHUNKS
SLOTS = 4
LEAD = 3
W_IN = [(3 * GW, "T"), (4 * GW, "T"), (6 * GW, "N"), (5 * GW, "N"), (7 * GW + FCOLS, "N"),
        (8 * GW + FCOLS, "N"), (2 * GW, "N"), (GW, "T"), (0, "N")]
GQ, GK, GROT, GVF, GVR, GGR, GSV, GSU, GPOOL = range(9)
NIN = len(W_IN)
IN_BANK = [2, 0, 2, 0, 2, 0, 2, 0, 4]
SETS = ((2, 3, 6, 7), (0, 1, 4, 5))
UD = 4 + 4 * 8
GROUPS = NIN + UD
NCH = GROUPS * CHUNKS
MIX_ORDER = [8, 9, 10, 11, 12, 13, 14, 15, 4, 5, 6, 7, 0, 1, 2, 3]
T_ID, T_ONE, T_TRI, T_NTRI, T_MASK, T_COS, T_SIN, T_EPS = 0, 128, 256, 512, 768, 1024, 1088, 1152
T_DEC = 1156
T_BAND = T_DEC + NH * S
T_ALL = T_BAND + 4 * 3 * P


def constants():
    t = np.zeros((P, T_ALL), np.float32)
    i = np.arange(P)
    upper = (i[:, None] <= i[None, :]).astype(np.float32)
    t[:, T_ID:T_ID + P] = np.eye(P)
    t[:, T_ONE:T_ONE + P] = 1
    t[:, T_TRI:T_TRI + S] = np.concatenate([upper, np.ones((P, P))], 1)
    t[:, T_NTRI:T_NTRI + S] = -t[:, T_TRI:T_TRI + S]
    t[:, T_MASK + P:T_MASK + 2 * P] = np.where(upper.T > 0, 0, NEG_BIG)
    half = RQK // 2
    inv = np.exp(-(np.arange(half, dtype=np.float32) / half) * np.float32(np.log(10000.0))).astype(np.float32)
    ang = (np.arange(S, dtype=np.float32)[:, None] * inv).astype(np.float64)
    for n in range(NT):
        t[:, T_COS + n * half:T_COS + (n + 1) * half] = np.cos(ang[n * P:(n + 1) * P])
        t[:, T_SIN + n * half:T_SIN + (n + 1) * half] = np.sin(ang[n * P:(n + 1) * P])
    t[:, T_EPS] = EPS
    l = np.arange(S)
    for h in range(NH):
        gamma = 1.0 - 2.0 ** (-5.0 - h)
        d = l[None, :] - i[:, None]
        t[:, T_DEC + h * S:T_DEC + (h + 1) * S] = np.where(d >= 0, gamma ** np.maximum(d, 0), 0) * RQK ** -0.5
    for n, w in enumerate(WINDOWS):
        for b, (t0, s0) in enumerate(((0, 0), (0, P), (P, P))):
            tt, ss = t0 + i[:, None], s0 + i[None, :]
            inside = (tt <= ss) & (tt > ss - w)
            at = T_BAND + (n * 3 + b) * P
            t[:, at:at + P] = inside / np.minimum(ss + 1, w) - (tt == ss)
    return t


class Signal:

    def __init__(self, sem, per, credit=0):
        self.sem, self.per, self.credit = sem, per, credit

    def at(self, layer, k):
        return layer * self.per + (k + self.credit)


def trunk(nc, x, w_in, w_out, w_ff1, w_ff2, tables, gain0, gains, fox_b, pool_w, pool_scale,
          sgu_g, sgu_w, sgu_b, ret_g, out):
    F, R = mybir.dt.float32, mybir.dt.float32r
    ALU, ACT, AX = mybir.AluOpType, mybir.ActivationFunctionType, mybir.AxisListType
    ds = bass.ds

    by_chunk = lambda w: w.rearrange("l (c t p) n -> (l c) p t n", t=CK, p=P)
    w_in_v, w_out_v, ff1_v, ff2_v = by_chunk(w_in), by_chunk(w_out), by_chunk(w_ff1), by_chunk(w_ff2)

    ctx = ExitStack()
    with ctx:
        def sb(name, shape, dt=F):
            return ctx.enter_context(nc.sbuf_tensor(name, shape, dt))

        def sig(name, per=1, credit=0):
            return Signal(ctx.enter_context(nc.semaphore(name)), per, credit)

        stage = sb("stage", [P, SLOTS, CK, CW + FCOLS])
        w_hi = sb("w_hi", [P, SLOTS, CK, CW + FCOLS], R)
        w_lo = sb("w_lo", [P, SLOTS, CK, CW + FCOLS], R)
        XN = sb("XN", [P, KT, 2 * S], R)
        FT = sb("FT", [P, KT, 2 * S], R)
        hT = sb("hT", [P, KT, S])
        tab = sb("tab", [P, T_ALL])
        ident_r = sb("ident_r", [P, P], R)
        A1 = sb("A1", [P, 2048])
        A2 = sb("A2", [P, 2048])
        A3 = sb("A3", [P, 2048])
        A4 = sb("A4", [P, 6 * 256])
        A5 = sb("A5", [P, 6 * 256])
        v_fox = sb("v_fox", [P, NT, GW])
        A6 = sb("A6", [P, 1024])
        rms = sb("rms", [P, S])
        rms2 = sb("rms2", [P, S])
        sq_acc = sb("sq_acc", [P, 2, S])
        sq = sb("sq", [P, 2, S])
        mean, root = sq[:, 0, :], sq[:, 1, :]
        rms_col = sb("rms_col", [P, NT])
        gain_first = sb("gain_first", [P, KT])
        gain = sb("gain", [P, 2, KT])
        fox_bias = sb("fox_bias", [P, NH])
        pscale = sb("pscale", [P, 4])
        pw = sb("pw", [P, 4, P])
        ws = sb("ws", [P, NH, P])
        wsT = sb("wsT", [P, NH, P])
        sbias = sb("sbias", [P, NH, P])
        sgain = sb("sgain", [P, GW])
        rgain = sb("rgain", [P, GW])
        forget = sb("forget", [P, NT, NH])
        f_abs = sb("f_abs", [P, NT, NH])
        f_min = sb("f_min", [P, NT, NH])
        cum_q = sb("cum_q", [P, NT, NH])
        smax = sb("smax", [P, NT * NH])
        ssum = sb("ssum", [P, NT * NH])
        hn = sb("hn", [P, 4, NT * NH])
        PS = ctx.enter_context(nc.psum_tensor("PS", [P, 8, 512], F))

        ident = tab[:, T_ID:T_ID + P]
        ones = tab[:, T_ONE:T_ONE + P]
        tri = tab[:, T_TRI:T_TRI + P]
        ntri = tab[:, T_NTRI:T_NTRI + S]
        mask = tab[:, T_MASK:T_MASK + S]
        eps = tab[:, T_EPS:T_EPS + 1]
        half = RQK // 2
        rot_table = lambda at: tab[:, at:at + NT * half].rearrange("p (t d) -> p t d", t=NT)\
            .unsqueeze(2).to_broadcast([P, NT, 2 * NH, half])
        decay = tab[:, T_DEC:T_DEC + NH * S].rearrange("p (h l) -> p h l", h=NH)
        band = tab[:, T_BAND:T_ALL].rearrange("p (w b s) -> p w b s", w=4, b=3)

        x_nat = [A1, A2]
        tmp = A1[:, 0:1024].rearrange("p (a t s) -> p a t s", a=2, t=2)
        up = A1[:, 1024:2048].rearrange("p (a t s) -> p a t s", a=2, t=2)
        down = A2[:, 0:1024].rearrange("p (a t s) -> p a t s", a=2, t=2)
        qT = A1[:, 0:1024].rearrange("p (h s) -> p h s", h=NH)
        kT = A1[:, 1024:2048].rearrange("p (h s) -> p h s", h=NH)
        gv = A1[:, 0:1024].rearrange("p (t n) -> p t n", t=NT)
        uT = A1[:, 1024:2048].rearrange("p (h s) -> p h s", h=NH)
        qk = A2[:, 0:1024].rearrange("p (t n) -> p t n", t=NT)
        rot = A2[:, 1024:2048].rearrange("p (t n) -> p t n", t=NT)
        swish = A2[:, 0:1024].rearrange("p (t n) -> p t n", t=NT)
        a_nat = A2[:, 1024:2048].rearrange("p (t n) -> p t n", t=NT)
        rot_tmp = A3[:, 0:512]
        rotT = A3[0:RQK, :].rearrange("p (h s) -> p h s", h=2 * NH)
        sq_head = A3[:, 0:1024]
        zT = A3[:, 0:1024].rearrange("p (h s) -> p h s", h=NH)
        pT = A3[:, 1024:2048].rearrange("p (w s) -> p w s", w=4)
        probs = (A4[:, 0:512].rearrange("p (h k) -> p h k", h=NH),
                 A4[:, 512:1536].rearrange("p (h k) -> p h k", h=NH))
        ret_s = (A4[:, 0:1024].rearrange("p (h l) -> p h l", h=NH),
                 A4[:, 1024:1536].rearrange("p (h l) -> p h l", h=NH))
        probsT = (A5[:, 0:1024].rearrange("p (h q) -> p h q", h=NH),
                  A5[:, 1024:1536].rearrange("p (h q) -> p h q", h=NH))
        y_ret = A5[:, 0:1024].rearrange("p (t n) -> p t n", t=NT)
        forget_b = A6[:, :].rearrange("p (a n) -> p a n", a=NT * NH)
        v_ret = A6[:, :].rearrange("p (t n) -> p t n", t=NT)
        out_sb = [A1, A2]

        f32 = lambda ap: ap.bitcast(F)
        flat = lambda ap: ap.rearrange("p a b -> p (a b)")

        def banks(b, n=2, parts=P):
            return PS[0:parts, b:b + n, :].rearrange("p b n -> p (b n)")

        staged = [sig(f"staged{n}", 16 * NCH // SLOTS) for n in range(SLOTS)]
        hi_done = sig("hi_done", NCH)
        lo_done = sig("lo_done", NCH, SLOTS)
        chunk_used = sig("chunk_used", NCH, SLOTS)
        half_done = sig("half_done", UD)
        tmp_ready = sig("tmp_ready", 2 * UD)
        combined = sig("combined", 2 * UD, 4)
        ff_ready = sig("ff_ready", 2 * 16)
        ft_hi = sig("ft_hi", 8 * 5)
        ft_done = sig("ft_done", 8 * 5)
        h_done = sig("h_done", 2 * 20, 2)
        sq_ready = sig("sq_ready", 2)
        sq_step = sig("sq_step", 2 * 16)
        scaled = sig("scaled", 2 * 16)
        xn_hi = sig("xn_hi", 16)
        xn_done = sig("xn_done", 16)
        sum_ready = sig("sum_ready", 2)
        root_ready = sig("root_ready", 2)
        rms_step = sig("rms_step", 2 * 7)
        rms_turned = sig("rms_turned", 1)
        col_ready = sig("col_ready", 1)
        in_read_v = sig("in_read_v", 3)
        in_read_s = sig("in_read_s", 12)
        small = sig("small", 16 * 8)
        gate_z = sig("gate_z", 4)
        gate_e = sig("gate_e", 2)
        forget_ready = sig("forget_ready", 2)
        cum_psum = sig("cum_psum", 1)
        cum_ready = sig("cum_ready", 1)
        rot_step = sig("rot_step", 6)
        rot_turned = sig("rot_turned", 1)
        rot_ready = sig("rot_ready", 2)
        score_psum = sig("score_psum", 2)
        score_ready = sig("score_ready", 8)
        max_step = sig("max_step", 4)
        exp_ready = sig("exp_ready", 8)
        recip_ready = sig("recip_ready", 2)
        probs_ready = sig("probs_ready", 2)
        probs_turned = sig("probs_turned", 3)
        probsT_ready = sig("probsT_ready", 3)
        fox_psum = sig("fox_psum", 1)
        ret_psum = sig("ret_psum", 1)
        ret_decayed = sig("ret_decayed", 3)
        y_psum = sig("y_psum", 1)
        norm_step = sig("norm_step", 2 * 10)
        norm_sq = sig("norm_sq", 2)
        norm_root = sig("norm_root", 2)
        swish_gain = sig("swish_gain", 1)
        ret_out = sig("ret_out", 1)
        ret_turned = sig("ret_turned", 1)
        ws_turned = sig("ws_turned", 1)
        ws_ready = sig("ws_ready", 1)
        sv_ready = sig("sv_ready", 1)
        u_ready = sig("u_ready", 1)
        z_psum = sig("z_psum", 1)
        z_step = sig("z_step", 2)
        pool_psum = sig("pool_psum", 1)
        pT_ready = sig("pT_ready", 1)
        poolw_psum = sig("poolw_psum", 1)
        x_in = [sig("x_in0", 0), sig("x_in1", 0)]
        ident_in = sig("ident_in", 0)
        tab_in = sig("tab_in", 0)
        gain0_in = sig("gain0_in", 0)
        xT_psum = sig("xT_psum", 0)
        hT_first = sig("hT_first", 0)
        ident_r_ready = sig("ident_r_ready", 0)
        out_psum = sig("out_psum", 0)
        out_s = sig("out_s", 0)
        out_v = sig("out_v", 0)
        load_turn = sig("load_turn", 0)
        turn_start = sig("turn_start", 0)
        stored = sig("stored", 0)

        def group_done(layer, g):
            return chunk_used.at(layer, g * CHUNKS + CHUNKS)

        block = ctx.enter_context(nc.Block())

        def in_width(g):
            return CW + FCOLS if g == GROT else CW

        @block.sync
        def _(sp):
            def load_chunk(layer, g, c, src):
                sp.wait_ge(lo_done.sem, lo_done.at(layer, g * CHUNKS + (c + 1 - SLOTS)))
                sp.sem_inc(load_turn.sem, 1)
                width = src.shape[-1]
                sp.dma_start(stage[:, c % SLOTS, :, 0:width], src).then_inc(staged[c % SLOTS].sem, 16)

            def load_up(layer, q, gi):
                for c in range(CHUNKS):
                    load_chunk(layer, NIN + 4 + q * 8 + gi, c,
                               ff1_v[layer * CHUNKS + c, :, :, ds(q * D + gi * CW, CW)])

            def load_down(layer, q, gi):
                for c in range(CHUNKS):
                    load_chunk(layer, NIN + 8 + q * 8 + gi, c,
                               ff2_v[layer * (4 * CHUNKS) + q * CHUNKS + c, :, :, ds(gi * CW, CW)])

            sp.dma_start(tab[:, 0:T_TRI], tables[:, 0:T_TRI]).then_inc(ident_in.sem, 16)
            for t in range(NT):
                sp.dma_start(x_nat[t][:, :], x[t * P:(t + 1) * P, :]).then_inc(x_in[t].sem, 16)
            sp.dma_start(gain_first[:, :], gain0).then_inc(gain0_in.sem, 16)
            with sp.Fori(0, DEPTH) as layer:
                for g, (col, _) in enumerate(W_IN):
                    for c in range(CHUNKS):
                        load_chunk(layer, g, c, w_in_v[layer * CHUNKS + c, :, :, col:col + in_width(g)])
                    if g == GK:
                        sp.dma_start(gain[:, :, :], gains[layer]).then_inc(small.sem, 16)
                        sp.dma_start(fox_bias[:, :], fox_b[ds(layer, 1), :].to_broadcast([P, NH])).then_inc(small.sem, 16)
                        sp.dma_start(pscale[:, :], pool_scale[layer]).then_inc(small.sem, 16)
                        sp.dma_start(pw[:, :, :], pool_w[layer]).then_inc(small.sem, 16)
                        sp.dma_start(ws[:, :, :], sgu_w[layer]).then_inc(small.sem, 16)
                        sp.dma_start(flat(sbias[:, :, :]), sgu_b[ds(layer, 1), :].to_broadcast([P, GW])).then_inc(small.sem, 16)
                        sp.dma_start(sgain[:, :], sgu_g[ds(layer, 1), :].to_broadcast([P, GW])).then_inc(small.sem, 16)
                        sp.dma_start(rgain[:, :], ret_g[ds(layer, 1), :].to_broadcast([P, GW])).then_inc(small.sem, 16)
                with sp.Fori(0, 4) as gi:
                    for c in range(CHUNKS):
                        load_chunk(layer, gi + NIN, c,
                                   w_out_v[layer * CHUNKS + MIX_ORDER[CK * c] // CK, :, :, ds(gi * CW, CW)])
                with sp.Fori(0, 4) as q:
                    with sp.Fori(0, 4) as gi:
                        load_up(layer, q, gi)
                    with sp.Fori(0, 4) as gi:
                        load_down(layer, q, gi)
            for c in range(LEAD):
                load_chunk(DEPTH, 0, c, w_in_v[c, :, :, W_IN[0][0]:W_IN[0][0] + CW])
            for t in range(NT):
                for n in range(4):
                    piece = 4 * t + n
                    sp.wait_ge([out_s, out_v][piece % 2].sem, piece // 2 + 1)
                    sp.dma_start(out[t * P:(t + 1) * P, n * CW:(n + 1) * CW],
                                 out_sb[t][:, n * CW:(n + 1) * CW]).then_inc(stored.sem, 16)
            sp.wait_ge(stored.sem, 16 * 4 * NT)

        @block.tensor
        def _(pe):
            def chunk_ready(layer, g, c):
                pe.wait_ge(lo_done.sem, lo_done.at(layer, g * CHUNKS + (c + 1)))

            def wide_group(layer, u, parity, moving, ready, ready_at, order, at_chunk=None):
                for c in range(CHUNKS):
                    chunk_ready(layer, u + NIN, c)
                    pe.wait_ge(ready.sem, ready.at(layer, ready_at + (c + 1)))
                    for t in range(CK):
                        kt = order[CK * c + t]
                        first, last = c == 0 and t == 0, c == CHUNKS - 1 and t == CK - 1
                        for j in range(4):
                            if first and j % 2 == 0:
                                pe.wait_ge(combined.sem, combined.at(layer, u * 2 + (j // 2 + 1 - 4)))
                            bank = SETS[parity][j]
                            cols = slice(j * P, (j + 1) * P)
                            both = lambda start, stop, skip: pe.matmul(
                                PS[:, bank, :], w_hi[:, c % SLOTS, t, cols], moving[:, kt, :],
                                start=start, stop=stop, skip_group_check=skip)
                            small_part = lambda: pe.matmul(
                                PS[:, bank, 0:S], w_lo[:, c % SLOTS, t, cols], moving[:, kt, 0:S],
                                start=False, stop=False, skip_group_check=True)
                            if last:
                                small_part()
                                mm = both(False, True, False)
                                if j == 1:
                                    mm.then_inc(half_done.sem, 1)
                            else:
                                both(first, False, False)
                                mm = small_part()
                            if j == 3 and t == CK - 1:
                                mm.then_inc(chunk_used.sem, 1)
                    if at_chunk:
                        at_chunk(c)

            def narrow_T(layer, g, c):
                for t in range(CK):
                    kt = CK * c + t
                    for j in range(4):
                        bank, at = IN_BANK[g] + j // 2, (j % 2) * S
                        cols = slice(j * P, (j + 1) * P)
                        first, last = kt == 0, kt == KT - 1
                        dst = PS[:, bank, at:at + S]
                        pe.matmul(dst, w_hi[:, c % SLOTS, t, cols], XN[:, kt, 0:S],
                                  start=first and j % 2 == 0, stop=False, skip_group_check=True)
                        pe.matmul(dst, w_hi[:, c % SLOTS, t, cols], XN[:, kt, S:2 * S],
                                  start=False, stop=False, skip_group_check=True)
                        mm = pe.matmul(dst, w_lo[:, c % SLOTS, t, cols], XN[:, kt, 0:S],
                                       start=False, stop=last, skip_group_check=True)
                return mm

            def narrow_N(layer, g, c):
                off = FCOLS if g == GROT else 0
                for t in range(CK):
                    kt = CK * c + t
                    for n in range(NT):
                        x_hi = XN[:, kt, n * P:(n + 1) * P]
                        x_lo = XN[:, kt, S + n * P:S + (n + 1) * P]
                        jobs = [(PS[:, IN_BANK[g] + n, :], slice(off, off + CW))]
                        if g == GROT:
                            jobs.append((PS[:, 6 + n, 0:FCOLS], slice(0, FCOLS)))
                        for dst, cols in jobs:
                            hi, lo = w_hi[:, c % SLOTS, t, cols], w_lo[:, c % SLOTS, t, cols]
                            pe.matmul(dst, x_hi, hi, start=kt == 0, stop=False)
                            pe.matmul(dst, x_hi, lo, start=False, stop=False)
                            mm = pe.matmul(dst, x_lo, hi, start=False, stop=kt == KT - 1)
                return mm

            def sum_squares(bank, layer, m):
                pe.wait_ge(sq_ready.sem, sq_ready.at(layer, m + 1))
                pe.matmul(PS[:, bank, 0:S], ones, sq_acc[:, 0, :], start=True, stop=False)
                pe.matmul(PS[:, bank, 0:S], ones, sq_acc[:, 1, :], start=False, stop=True).then_inc(sum_ready.sem, 1)

            def turn_rms(bank, layer, k):
                pe.wait_ge(rms_step.sem, rms_step.at(layer, k))
                for n in range(NT):
                    mm = pe.matmul(PS[:, bank, n:n + 1], rms[0:1, n * P:(n + 1) * P], ones[0:1, 0:1],
                                   start=True, stop=True)
                mm.then_inc(rms_turned.sem, 1)

            def turn(dst, src):
                return pe.matmul(dst, src, ident, start=True, stop=True, is_transpose=True)

            def running_sums(layer):
                pe.wait_ge(forget_ready.sem, forget_ready.at(layer, 1))
                pe.matmul(PS[:, 7, 0:NH], tri, forget[:, 0, :], start=True, stop=True)
                pe.matmul(PS[:, 7, NH:2 * NH], ones, forget[:, 0, :], start=True, stop=False)
                pe.matmul(PS[:, 7, NH:2 * NH], tri, forget[:, 1, :], start=False, stop=True).then_inc(cum_psum.sem, 1)

            def turn_rotated(layer):
                pe.wait_ge(rot_step.sem, rot_step.at(layer, 6))
                pe.wait_ge(cum_ready.sem, cum_ready.at(layer, 1))
                pe.sem_inc(turn_start.sem, 1)
                for h in range(2 * NH):
                    for n in range(NT):
                        at = (2 * (h % 2) + n) * P
                        mm = turn(PS[0:RQK, 4 + h // 2, at:at + P], rot[:, n, h * RQK:(h + 1) * RQK])
                mm.then_inc(rot_turned.sem, 1)

            def fox_scores(layer, i):
                pe.wait_ge(forget_ready.sem, forget_ready.at(layer, 2))
                pe.wait_ge(in_read_v.sem, in_read_v.at(layer, 2))
                pe.wait_ge(rot_ready.sem, rot_ready.at(layer, 2))
                for h in range(NH):
                    q = qT[:, h, i * P:(i + 1) * P]
                    if i == 0:
                        dst = PS[:, 5, h * P:(h + 1) * P]
                        pe.matmul(dst, q, kT[:, h, 0:P], start=True, stop=False)
                        mm = pe.matmul(dst, forget_b[:, h, :], ntri[:, 0:P], start=False, stop=True)
                    else:
                        bank, at = 6 + h // 2, (h % 2) * S
                        pe.matmul(PS[:, bank, at:at + S], q, kT[:, h, :], start=True, stop=False)
                        pe.matmul(PS[:, bank, at + P:at + S], forget_b[:, NH + h, :], ntri[:, 0:P],
                                  start=False, stop=False, skip_group_check=True)
                        mm = pe.matmul(PS[:, bank, at:at + S], forget_b[:, h, :], ntri, start=False, stop=True)
                mm.then_inc(score_psum.sem, 1)

            def turn_probs(layer):
                for n, (bank, i, k) in enumerate(((5, 0, 0), (6, 1, 0), (7, 1, 1))):
                    pe.wait_ge(probs_ready.sem, probs_ready.at(layer, i + 1))
                    for h in range(NH):
                        mm = turn(PS[:, bank, h * P:(h + 1) * P], probs[i][:, h, k * P:(k + 1) * P])
                    mm.then_inc(probs_turned.sem, 1)

            def fox_output(layer):
                pe.wait_ge(probsT_ready.sem, probsT_ready.at(layer, 3))
                pe.wait_ge(in_read_s.sem, in_read_s.at(layer, 4))
                for h in range(NH):
                    bank, at = 5 + h // 2, (h % 2) * S
                    v0, v1 = (v_fox[:, n, h * HD:(h + 1) * HD] for n in range(NT))
                    pe.matmul(PS[:, bank, at:at + P], v0, probsT[0][:, h, 0:P], start=True, stop=True)
                    pe.matmul(PS[:, bank, at + P:at + S], v0, probsT[0][:, h, P:S], start=True, stop=False)
                    mm = pe.matmul(PS[:, bank, at + P:at + S], v1, probsT[1][:, h, :], start=False, stop=True)
                mm.then_inc(fox_psum.sem, 1)

            def ret_scores(layer):
                pe.wait_ge(ft_done.sem, ft_done.at(layer, 2))
                for h in range(NH):
                    q, k = rotT[:, h, :], rotT[:, NH + h, :]
                    bank, at = 4 if h < 2 else 7, (h % 2) * S
                    pe.matmul(PS[:, bank, at:at + S], k[:, 0:P], q, start=True, stop=True)
                for h in range(NH):
                    q, k = rotT[:, h, :], rotT[:, NH + h, :]
                    mm = pe.matmul(PS[:, 5, h * P:(h + 1) * P], k[:, P:S], q[:, P:S], start=True, stop=True)
                mm.then_inc(ret_psum.sem, 1)

            def ret_output(layer):
                pe.wait_ge(ret_decayed.sem, ret_decayed.at(layer, 3))
                pe.wait_ge(in_read_s.sem, in_read_s.at(layer, 6))
                for h in range(NH):
                    v0, v1 = (v_ret[:, n, h * HD:(h + 1) * HD] for n in range(NT))
                    cols = slice(h * P, (h + 1) * P)
                    pe.matmul(PS[:, 6, cols], ret_s[0][:, h, 0:P], v0, start=True, stop=True)
                    pe.matmul(PS[:, 7, cols], ret_s[0][:, h, P:S], v0, start=True, stop=False)
                    mm = pe.matmul(PS[:, 7, cols], ret_s[1][:, h, :], v1, start=False, stop=True)
                mm.then_inc(y_psum.sem, 1)

            def turn_ret(layer):
                pe.wait_ge(ret_out.sem, ret_out.at(layer, 1))
                for h in range(NH):
                    for n in range(NT):
                        at = (h % 2) * S + n * P
                        mm = turn(PS[:, 4 + h // 2, at:at + P], y_ret[:, n, h * HD:(h + 1) * HD])
                mm.then_inc(ret_turned.sem, 1)

            def turn_ws(layer):
                pe.wait_ge(small.sem, small.at(layer, 16 * 8))
                pe.wait_ge(ft_done.sem, ft_done.at(layer, 4))
                for h in range(NH):
                    mm = turn(PS[:, 4, h * P:(h + 1) * P], ws[:, h, :])
                mm.then_inc(ws_turned.sem, 1)

            def mix_positions(layer):
                pe.wait_ge(sv_ready.sem, sv_ready.at(layer, 1))
                pe.wait_ge(ws_ready.sem, ws_ready.at(layer, 1))
                for h in range(NH):
                    for n in range(NT):
                        at = (h % 2) * S + n * P
                        mm = pe.matmul(PS[:, 6 + h // 2, at:at + P], gv[:, n, h * HD:(h + 1) * HD], wsT[:, h, :],
                                       start=True, stop=True)
                mm.then_inc(z_psum.sem, 1)

            def pool_means(layer):
                pe.wait_ge(in_read_s.sem, in_read_s.at(layer, 12))
                for w in range(4):
                    bank, at = w // 2, (w % 2) * S
                    a0, a1 = (a_nat[:, n, w * P:(w + 1) * P] for n in range(NT))
                    pe.matmul(PS[:, bank, at:at + P], a0, band[:, w, 0, :], start=True, stop=True)
                    pe.matmul(PS[:, bank, at + P:at + S], a0, band[:, w, 1, :], start=True, stop=False)
                    mm = pe.matmul(PS[:, bank, at + P:at + S], a1, band[:, w, 2, :], start=False, stop=True)
                mm.then_inc(pool_psum.sem, 1)

            def pool_product(layer):
                pe.wait_ge(pT_ready.sem, pT_ready.at(layer, 1))
                for w in range(4):
                    mm = pe.matmul(PS[:, 4 + w // 2, (w % 2) * S:(w % 2 + 1) * S], pw[:, w, :], pT[:, w, :],
                                   start=True, stop=True)
                mm.then_inc(poolw_psum.sem, 1)

            pe.wait_ge(ident_in.sem, 16)
            for n in range(NT):
                pe.wait_ge(x_in[n].sem, 16)
            for i in range(KT // 2):
                for t in range(2):
                    for n in range(NT):
                        at = (2 * t + n) * P
                        mm = turn(PS[:, i, at:at + P], x_nat[n][:, (2 * i + t) * P:(2 * i + t + 1) * P])
                mm.then_inc(xT_psum.sem, 1)
            pe.wait_ge(tab_in.sem, 16)
            pe.wait_ge(hT_first.sem, KT // 2)

            with pe.Fori(0, DEPTH) as layer:
                for g in range(NIN):
                    for c in range(CHUNKS):
                        chunk_ready(layer, g, c)
                        if g == 0:
                            pe.wait_ge(xn_done.sem, xn_done.at(layer, c + 1))
                        if c == 0:
                            if g == 0:
                                pe.wait_ge(combined.sem, combined.at(layer, -2))
                            if g == 1:
                                pe.wait_ge(combined.sem, combined.at(layer, 0))
                            if g == GROT:
                                pe.wait_ge(in_read_v.sem, in_read_v.at(layer, 1))
                            if g == GVF:
                                pe.wait_ge(in_read_v.sem, in_read_v.at(layer, 2))
                            if GVR <= g <= GSU:
                                pe.wait_ge(in_read_s.sem, in_read_s.at(layer, 2 * (g - 3)))
                            if g == GPOOL:
                                pe.wait_ge(ws_ready.sem, ws_ready.at(layer, 1))
                        mm = (narrow_T if W_IN[g][1] == "T" else narrow_N)(layer, g, c)
                        mm.then_inc(chunk_used.sem, 1)
                        if (g, c) == (0, 5):
                            sum_squares(4, layer, 0)
                        if (g, c) == (0, 7):
                            turn_rms(5, layer, 6)
                        if (g, c) == (3, 3):
                            running_sums(layer)
                        if (g, c) == (3, 6):
                            turn_rotated(layer)
                        if (g, c) == (4, 0):
                            fox_scores(layer, 0)
                        if (g, c) == (4, 1):
                            fox_scores(layer, 1)
                        if (g, c) == (4, 5):
                            turn_probs(layer)
                        if (g, c) == (5, 0):
                            fox_output(layer)
                        if (g, c) == (5, 3):
                            ret_scores(layer)
                        if (g, c) == (5, 6):
                            ret_output(layer)
                        if (g, c) == (6, 6):
                            turn_ret(layer)
                        if (g, c) == (7, 3):
                            turn_ws(layer)
                        if (g, c) == (8, 3):
                            mix_positions(layer)

                def pool_steps(c):
                    if c == 0:
                        pool_means(layer)
                    if c == 2:
                        pool_product(layer)

                natural = list(range(KT))
                for gi in range(4):
                    if gi == 0:
                        pe.wait_ge(z_step.sem, z_step.at(layer, 1))
                    wide_group(layer, gi, gi % 2, FT, ft_done, 0, MIX_ORDER, pool_steps if gi == 0 else None)

                def mlp_sum(c):
                    if c == 5:
                        sum_squares(4, layer, 1)

                for gi in range(4):
                    if gi == 1:
                        pe.wait_ge(rms_step.sem, rms_step.at(layer, 6 + 7))
                    wide_group(layer, gi + 4, gi % 2, XN, xn_done, 8, natural, mlp_sum if gi == 0 else None)
                with pe.Fori(0, 3) as q:
                    with pe.Fori(0, 2) as i:
                        for s in range(2):
                            wide_group(layer, q * 8 + i * 2 + (8 + s), s, FT, ft_done, q * 8 + 8, natural)
                    with pe.Fori(0, 2) as i:
                        for s in range(2):
                            wide_group(layer, q * 8 + i * 2 + (12 + s), s, XN, xn_done, 8, natural)
                with pe.Fori(0, 2) as i:
                    for s in range(2):
                        wide_group(layer, i * 2 + (32 + s), s, FT, ft_done, 32, natural)

            sum_squares(2, DEPTH, 0)
            pe.wait_ge(ident_r_ready.sem, 1)
            pe.wait_ge(xn_done.sem, xn_done.at(DEPTH, 8))
            out_banks = [6, 7, 0, 1, 4, 5, 6, 7]
            for piece in range(8):
                n, g = divmod(piece, 4)
                if piece >= 6:
                    pe.wait_ge([out_s, out_v][piece % 2].sem, (piece - 6) // 2 + 1)
                for j in range(4):
                    dst = PS[:, out_banks[piece], j * P:(j + 1) * P]
                    pe.matmul(dst, XN[:, 4 * g + j, n * P:(n + 1) * P], ident_r[:, :], start=True, stop=False)
                    mm = pe.matmul(dst, XN[:, 4 * g + j, S + n * P:S + (n + 1) * P], ident_r[:, :],
                                   start=False, stop=True)
                mm.then_inc(out_psum.sem, 1)
                if piece == 3:
                    turn_rms(3, DEPTH, 6)

        @block.scalar
        def _(act):
            def split_hi(layer, g, k, width=CW):
                slot = k % SLOTS
                act.wait_ge(staged[slot].sem, staged[slot].at(layer, g * 32 + (k // SLOTS + 1) * 16))
                act.wait_ge(chunk_used.sem, chunk_used.at(layer, g * CHUNKS + (k + 1 - SLOTS)))
                act.activation(w_hi[:, slot, :, 0:width], stage[:, slot, :, 0:width], ACT.Copy).then_inc(hi_done.sem, 1)

            def splits(layer, g, at_chunk=None, widths=None):
                for c in range(CHUNKS):
                    split_hi(layer, g, c + LEAD, (widths or {}).get(c + LEAD >= CHUNKS, CW))
                    if at_chunk:
                        at_chunk(c)

            def read_tmp(layer, u, parity, p):
                if p == 0:
                    act.wait_ge(half_done.sem, half_done.at(layer, u + 1))
                else:
                    act.wait_ge(chunk_used.sem, group_done(layer, u + NIN))
                act.wait_ge(combined.sem, combined.at(layer, u * 2 + (p - 1)))
                b = SETS[parity][2 * p]
                act.activation(tmp[:, p, :, :], PS[:, b:b + 2, S:2 * S], ACT.Copy).then_inc(tmp_ready.sem, 1)

            def evacuate_up(layer, u, parity, q, gi):
                for p in range(2):
                    read_tmp(layer, u, parity, p)
                for p in range(2):
                    act.wait_ge(ff_ready.sem, ff_ready.at(layer, q * 8 + gi * 2 + (p + 1)))
                    act.activation(FT[:, ds(gi * 4 + 2 * p, 2), 0:S], up[:, p, :, :], ACT.Copy).then_inc(ft_hi.sem, 1)

            def norm_hi(g_cols, tile0):
                for t in range(2):
                    a = act.activation(XN[:, ds(tile0 + t, 1), 0:S].rearrange("p o s -> p (o s)"),
                                       hT[:, ds(tile0 + t, 1), :].rearrange("p o s -> p (o s)"), ACT.Copy,
                                       scale=g_cols[:, ds(tile0 + t, 1)])
                a.then_inc(xn_hi.sem, 1)

            def evacuate_down(layer, u, parity, f, gi, gain_row=None):
                for p in range(2):
                    read_tmp(layer, u, parity, p)
                if gain_row is not None:
                    for p in range(2):
                        act.wait_ge(h_done.sem, h_done.at(layer, f * 8 + gi * 2 + (p + 1)))
                        norm_hi(gain[:, gain_row, :], gi * 4 + 2 * p)

            def root_of_mean(layer, m, bank):
                act.wait_ge(sum_ready.sem, sum_ready.at(layer, m + 1))
                act.activation(root, PS[:, bank, 0:S], ACT.Sqrt, scale=1.0 / D, bias=eps).then_inc(root_ready.sem, 1)

            def read_natural(layer, g, dst, func):
                act.wait_ge(chunk_used.sem, group_done(layer, g))
                for n in range(NT):
                    act.activation(dst[:, n, :], PS[:, IN_BANK[g] + n, :], func, scale=rms_col[:, n:n + 1])\
                       .then_inc(in_read_s.sem, 1)

            def head_norm(layer, k, src):
                act.wait_ge(norm_step.sem, norm_step.at(layer, 10 * k + 3))
                act.activation(sq_head, src.rearrange("p t n -> p (t n)"), ACT.Square).then_inc(norm_sq.sem, 1)
                act.wait_ge(norm_step.sem, norm_step.at(layer, 10 * k + 4))
                act.activation(hn[:, 1, :], hn[:, 0, :], ACT.Sqrt, scale=1.0 / HD, bias=eps).then_inc(norm_root.sem, 1)

            def ft_hi_from(src, tile0):
                act.activation(FT[:, tile0:tile0 + 2, 0:S], src, ACT.Copy).then_inc(ft_hi.sem, 1)

            act.dma_start(tab[:, T_TRI:T_ALL], tables[:, T_TRI:T_ALL]).then_inc(tab_in.sem, 16)
            act.wait_ge(ident_in.sem, 16)
            act.activation(ident_r[:, :], ident, ACT.Copy).then_inc(ident_r_ready.sem, 1)
            for c in range(LEAD):
                split_hi(0, 0, c)
            act.wait_ge(gain0_in.sem, 16)
            for i in range(KT // 2):
                act.wait_ge(hT_first.sem, i + 1)
                norm_hi(gain_first, 2 * i)
            act.wait_ge(tab_in.sem, 16)

            with act.Fori(0, DEPTH) as layer:
                for g in range(NIN):
                    def steps(c):
                        if (g, c) == (0, 5):
                            root_of_mean(layer, 0, 4)
                        if (g, c) == (2, 7):
                            act.wait_ge(col_ready.sem, col_ready.at(layer, 1))
                            act.wait_ge(small.sem, small.at(layer, 16 * 8))
                            read_natural(layer, GROT, qk, ACT.Copy)
                            act.wait_ge(gate_z.sem, gate_z.at(layer, 3))
                            act.activation(f_abs[:, :, :], f_abs[:, :, :], ACT.Exp, scale=-1.0).then_inc(gate_e.sem, 1)
                            act.wait_ge(gate_e.sem, gate_e.at(layer, 1))
                            act.activation(f_abs[:, :, :], f_abs[:, :, :], ACT.Ln, bias=1.0).then_inc(gate_e.sem, 1)
                        if (g, c) == (3, 6):
                            act.wait_ge(rot_turned.sem, rot_turned.at(layer, 1))
                            for n in range(2):
                                act.activation(flat(rotT[:, 4 * n:4 * n + 4, :]), banks(4 + 2 * n, 2, RQK), ACT.Copy)\
                                   .then_inc(rot_ready.sem, 1)
                        if (g, c) == (3, 7):
                            read_natural(layer, GVF, v_fox, ACT.Copy)
                        if (g, c) in ((4, 1), (4, 2)):
                            i = c - 1
                            act.wait_ge(max_step.sem, max_step.at(layer, 2 * i + 2))
                            for h in range(NH):
                                k = i * NH + h
                                act.activation(probs[i][:, h, :], probs[i][:, h, :], ACT.Exp, bias=smax[:, k:k + 1],
                                               accum_out=ssum[:, k:k + 1]).then_inc(exp_ready.sem, 1)
                        if (g, c) == (4, 5):
                            for n, dst in enumerate((probsT[0][:, :, 0:P], probsT[0][:, :, P:S], probsT[1])):
                                act.wait_ge(probs_turned.sem, probs_turned.at(layer, n + 1))
                                act.activation(dst, PS[:, 5 + n, :].rearrange("p (h q) -> p h q", h=NH), ACT.Copy)\
                                   .then_inc(probsT_ready.sem, 1)
                        if (g, c) == (4, 7):
                            read_natural(layer, GVR, v_ret, ACT.Copy)
                        if (g, c) == (5, 0):
                            act.wait_ge(fox_psum.sem, fox_psum.at(layer, 1))
                            for n in range(2):
                                ft_hi_from(PS[:, 5 + n, :].rearrange("p (h s) -> p h s", h=2), 8 + 2 * n)
                        if (g, c) == (5, 7):
                            read_natural(layer, GGR, swish, ACT.Silu)
                            head_norm(layer, 0, y_ret)
                        if (g, c) == (6, 6):
                            act.wait_ge(ret_turned.sem, ret_turned.at(layer, 1))
                            for n in range(2):
                                ft_hi_from(PS[:, 4 + n, :].rearrange("p (h s) -> p h s", h=2), 12 + 2 * n)
                        if (g, c) == (6, 7):
                            read_natural(layer, GSV, gv, ACT.Gelu_apprx_tanh)
                            head_norm(layer, 1, gv)
                        if (g, c) == (7, 7):
                            act.wait_ge(in_read_v.sem, in_read_v.at(layer, 3))
                            act.activation(flat(uT), flat(uT), ACT.Gelu_apprx_tanh).then_inc(u_ready.sem, 1)
                        if (g, c) == (8, 3):
                            act.wait_ge(z_step.sem, z_step.at(layer, 2))
                            for n in range(2):
                                ft_hi_from(zT[:, 2 * n:2 * n + 2, :], 4 + 2 * n)
                        if (g, c) == (8, 7):
                            read_natural(layer, GPOOL, a_nat, ACT.Copy)

                    splits(layer, g, steps, {False: in_width(g), True: in_width(g + 1)})

                def pool_steps(c):
                    if c == 0:
                        act.wait_ge(pool_psum.sem, pool_psum.at(layer, 1))
                        act.activation(flat(pT), banks(0), ACT.Copy).then_inc(pT_ready.sem, 1)
                    if c == 2:
                        act.wait_ge(poolw_psum.sem, poolw_psum.at(layer, 1))
                        for w in range(4):
                            a = act.activation(FT[:, w, 0:S], PS[:, 4 + w // 2, (w % 2) * S:(w % 2 + 1) * S], ACT.Copy,
                                               scale=pscale[:, w:w + 1])
                            if w % 2:
                                a.then_inc(ft_hi.sem, 1)

                def mlp_root(c):
                    if c == 5:
                        root_of_mean(layer, 1, 4)

                for gi in range(4):
                    splits(layer, NIN + gi, pool_steps if gi == 0 else None)
                    evacuate_down(layer, gi, gi % 2, 0, gi, 0)
                for gi in range(4):
                    splits(layer, NIN + 4 + gi, mlp_root if gi == 0 else None)
                    evacuate_up(layer, gi + 4, gi % 2, 0, gi)
                with act.Fori(0, 3) as q:
                    with act.Fori(0, 2) as i:
                        for s in range(2):
                            splits(layer, q * 8 + i * 2 + (NIN + 8 + s))
                            evacuate_down(layer, q * 8 + i * 2 + (8 + s), s, q + 1, i * 2 + s)
                    with act.Fori(0, 2) as i:
                        for s in range(2):
                            splits(layer, q * 8 + i * 2 + (NIN + 12 + s))
                            evacuate_up(layer, q * 8 + i * 2 + (12 + s), s, q + 1, i * 2 + s)
                with act.Fori(0, 2) as i:
                    for s in range(2):
                        splits(layer, i * 2 + (NIN + 32 + s))
                        evacuate_down(layer, i * 2 + (32 + s), s, 4, i * 2 + s, 1)

            root_of_mean(DEPTH, 0, 2)
            act.wait_ge(col_ready.sem, col_ready.at(DEPTH, 1))
            for piece in range(0, 8, 2):
                n, g = divmod(piece, 4)
                act.wait_ge(out_psum.sem, piece + 1)
                act.activation(out_sb[n][:, g * CW:(g + 1) * CW], PS[:, [6, 7, 0, 1, 4, 5, 6, 7][piece], :], ACT.Copy,
                               scale=rms_col[:, n:n + 1]).then_inc(out_s.sem, 1)

        @block.vector
        def _(dve):
            def split_lo(layer, g, k, width=CW):
                slot = k % SLOTS
                dve.wait_ge(hi_done.sem, hi_done.at(layer, g * CHUNKS + (k + 1)))
                dve.tensor_tensor(w_lo[:, slot, :, 0:width], stage[:, slot, :, 0:width],
                                  f32(w_hi[:, slot, :, 0:width]), ALU.subtract).then_inc(lo_done.sem, 1)

            def splits(layer, g, at_chunk=None, widths=None):
                for c in range(CHUNKS):
                    split_lo(layer, g, c + LEAD, (widths or {}).get(c + LEAD >= CHUNKS, CW))
                    if at_chunk:
                        at_chunk(c)

            def evacuate_up(layer, u, parity, q, gi):
                for p in range(2):
                    b = SETS[parity][2 * p]
                    dve.wait_ge(tmp_ready.sem, tmp_ready.at(layer, u * 2 + (p + 1)))
                    dve.tensor_tensor(up[:, p, :, :], PS[:, b:b + 2, 0:S], tmp[:, p, :, :], ALU.add)\
                       .then_inc(combined.sem, 1)
                    dve.wait_ge(combined.sem, combined.at(layer, u * 2 + (p + 1)))
                    dve.scalar_tensor_tensor(up[:, p, :, :], up[:, p, :, :], 0.0, up[:, p, :, :], ALU.max, ALU.mult)\
                       .then_inc(ff_ready.sem, 1)
                for p in range(2):
                    dve.wait_ge(ft_hi.sem, ft_hi.at(layer, q * 8 + gi * 2 + (8 + p + 1)))
                    tiles = ds(gi * 4 + 2 * p, 2)
                    dve.tensor_tensor(FT[:, tiles, S:2 * S], up[:, p, :, :], f32(FT[:, tiles, 0:S]), ALU.subtract)\
                       .then_inc(ft_done.sem, 1)

            def norm_lo(g_cols, tile0):
                for t in range(2):
                    one = lambda ap: ap.rearrange("p o s -> p (o s)")
                    v = dve.scalar_tensor_tensor(one(XN[:, ds(tile0 + t, 1), S:2 * S]), one(hT[:, ds(tile0 + t, 1), :]),
                                                 g_cols[:, ds(tile0 + t, 1)], one(f32(XN[:, ds(tile0 + t, 1), 0:S])),
                                                 ALU.mult, ALU.subtract)
                v.then_inc(xn_done.sem, 1)

            def evacuate_down(layer, u, parity, f, gi, gain_row=None, norm_at=0):
                for p in range(2):
                    b = SETS[parity][2 * p]
                    dve.wait_ge(tmp_ready.sem, tmp_ready.at(layer, u * 2 + (p + 1)))
                    dve.wait_ge(h_done.sem, h_done.at(layer, f * 8 + gi * 2 + (p - 1)))
                    dve.tensor_tensor(down[:, p, :, :], PS[:, b:b + 2, 0:S], tmp[:, p, :, :], ALU.add)\
                       .then_inc(combined.sem, 1)
                if gain_row is not None:
                    for p in range(2):
                        dve.wait_ge(xn_hi.sem, xn_hi.at(layer, gi * 2 + (norm_at + p + 1)))
                        norm_lo(gain[:, gain_row, :], gi * 4 + 2 * p)

            def inverse_rms(layer, m, bank):
                k = [7 * m]

                def after():
                    k[0] += 1
                    return rms_step.at(layer, k[0])
                dve.wait_ge(root_ready.sem, root_ready.at(layer, m + 1))
                dve.tensor_scalar(mean, PS[:, bank, 0:S], 1.0 / D, EPS, ALU.mult, ALU.add).then_inc(rms_step.sem, 1)
                after()
                dve.reciprocal(rms[:, :], root).then_inc(rms_step.sem, 1)
                dve.wait_ge(rms_step.sem, after())
                dve.tensor_tensor(root, rms[:, :], rms[:, :], ALU.mult).then_inc(rms_step.sem, 1)
                dve.wait_ge(rms_step.sem, after())
                dve.tensor_tensor(root, root, mean, ALU.mult).then_inc(rms_step.sem, 1)
                dve.wait_ge(rms_step.sem, after())
                dve.tensor_scalar(root, root, -0.5, 1.5, ALU.mult, ALU.add).then_inc(rms_step.sem, 1)
                dve.wait_ge(rms_step.sem, after())
                dve.tensor_tensor(rms[:, :], rms[:, :], root, ALU.mult).then_inc(rms_step.sem, 1)
                dve.wait_ge(rms_step.sem, after())
                dve.tensor_tensor(rms2[:, :], rms[:, :], rms[:, :], ALU.mult).then_inc(rms_step.sem, 1)

            def rms_columns(layer, bank):
                dve.wait_ge(rms_turned.sem, rms_turned.at(layer, 1))
                dve.tensor_copy(rms_col[:, :], PS[:, bank, 0:NT]).then_inc(col_ready.sem, 1)

            wide_rms = rms[:, :].unsqueeze(1).to_broadcast([P, 4, S])
            heads = lambda ap: ap.rearrange("p (a n) -> p a n", a=NT * NH)

            def spread(col, n=NT * NH, width=P):
                return col.unsqueeze(2).to_broadcast([P, n, width])

            def head_norm(layer, k, src, dst):
                n = [10 * k]

                def after():
                    n[0] += 1
                    return norm_step.at(layer, n[0])
                dve.tensor_reduce(hn[:, 0, :], src, AX.X, ALU.add).then_inc(norm_step.sem, 1)
                dve.wait_ge(norm_step.sem, after())
                dve.tensor_scalar(hn[:, 2, :], hn[:, 0, :], 1.0 / HD, None, ALU.mult).then_inc(norm_step.sem, 1)
                dve.wait_ge(norm_step.sem, after())
                dve.tensor_tensor(dst, src, spread(hn[:, 2, :]), ALU.subtract).then_inc(norm_step.sem, 1)
                after()
                dve.wait_ge(norm_sq.sem, norm_sq.at(layer, k + 1))
                dve.tensor_reduce(hn[:, 0, :], heads(sq_head), AX.X, ALU.add).then_inc(norm_step.sem, 1)
                dve.wait_ge(norm_step.sem, after())
                dve.tensor_scalar(hn[:, 2, :], hn[:, 0, :], 1.0 / HD, EPS, ALU.mult, ALU.add).then_inc(norm_step.sem, 1)
                after()
                dve.wait_ge(norm_root.sem, norm_root.at(layer, k + 1))
                dve.reciprocal(hn[:, 1, :], hn[:, 1, :]).then_inc(norm_step.sem, 1)
                dve.wait_ge(norm_step.sem, after())
                dve.tensor_tensor(hn[:, 3, :], hn[:, 1, :], hn[:, 1, :], ALU.mult).then_inc(norm_step.sem, 1)
                dve.wait_ge(norm_step.sem, after())
                dve.tensor_tensor(hn[:, 3, :], hn[:, 3, :], hn[:, 2, :], ALU.mult).then_inc(norm_step.sem, 1)
                dve.wait_ge(norm_step.sem, after())
                dve.scalar_tensor_tensor(hn[:, 3, :], hn[:, 3, :], 3.0, hn[:, 1, :], ALU.subtract, ALU.mult)\
                   .then_inc(norm_step.sem, 1)
                dve.wait_ge(norm_step.sem, after())
                dve.scalar_tensor_tensor(dst, dst, -0.5, spread(hn[:, 3, :]), ALU.mult, ALU.mult)\
                   .then_inc(norm_step.sem, 1)

            def ft_lo(layer, k, src, tile0):
                dve.wait_ge(ft_hi.sem, ft_hi.at(layer, k))
                dve.tensor_tensor(FT[:, tile0:tile0 + 2, S:2 * S], src, f32(FT[:, tile0:tile0 + 2, 0:S]), ALU.subtract)\
                   .then_inc(ft_done.sem, 1)

            dve.sem_inc(lo_done.sem, SLOTS)
            dve.sem_inc(chunk_used.sem, SLOTS)
            dve.sem_inc(combined.sem, 4)
            dve.sem_inc(h_done.sem, 2)
            for c in range(LEAD):
                split_lo(0, 0, c)
            dve.wait_ge(gain0_in.sem, 16)
            for i in range(KT // 2):
                dve.wait_ge(xT_psum.sem, i + 1)
                dve.tensor_copy(flat(hT[:, 2 * i:2 * i + 2, :]), PS[:, i, :]).then_inc(hT_first.sem, 1)
                if i:
                    dve.wait_ge(xn_hi.sem, i)
                    norm_lo(gain_first, 2 * i - 2)
            dve.wait_ge(xn_hi.sem, KT // 2)
            norm_lo(gain_first, KT - 2)
            dve.wait_ge(tab_in.sem, 16)

            with dve.Fori(0, DEPTH) as layer:
                for g in range(NIN):
                    def steps(c):
                        if (g, c) == (0, 5):
                            inverse_rms(layer, 0, 4)
                        if (g, c) == (0, 7):
                            rms_columns(layer, 5)
                            dve.wait_ge(chunk_used.sem, group_done(layer, GQ))
                            dve.scalar_tensor_tensor(qT, banks(IN_BANK[GQ]).rearrange("p (h s) -> p h s", h=NH), Q_SCALE,
                                                     wide_rms, ALU.mult, ALU.mult).then_inc(in_read_v.sem, 1)
                        if (g, c) == (1, 7):
                            dve.wait_ge(chunk_used.sem, group_done(layer, GK))
                            dve.tensor_tensor(kT, banks(IN_BANK[GK]).rearrange("p (h s) -> p h s", h=NH), wide_rms,
                                              ALU.mult).then_inc(in_read_v.sem, 1)
                        if (g, c) == (2, 7):
                            dve.wait_ge(chunk_used.sem, group_done(layer, GROT))
                            dve.wait_ge(small.sem, small.at(layer, 16 * 8))
                            dve.wait_ge(col_ready.sem, col_ready.at(layer, 1))
                            for n in range(NT):
                                dve.scalar_tensor_tensor(f_min[:, n, :], PS[:, 6 + n, 0:NH], rms_col[:, n:n + 1],
                                                         fox_bias[:, :], ALU.mult, ALU.add).then_inc(gate_z.sem, 1)
                            dve.wait_ge(gate_z.sem, gate_z.at(layer, 2))
                            dve.scalar_tensor_tensor(f_abs[:, :, :], f_min[:, :, :], -1.0, f_min[:, :, :], ALU.mult, ALU.max)\
                               .then_inc(gate_z.sem, 1)
                            dve.wait_ge(gate_z.sem, gate_z.at(layer, 3))
                            dve.tensor_scalar(f_min[:, :, :], f_min[:, :, :], 0.0, None, ALU.min).then_inc(gate_z.sem, 1)
                            dve.wait_ge(gate_z.sem, gate_z.at(layer, 4))
                            dve.wait_ge(gate_e.sem, gate_e.at(layer, 2))
                            dve.tensor_tensor(forget[:, :, :], f_min[:, :, :], f_abs[:, :, :], ALU.subtract)\
                               .then_inc(forget_ready.sem, 1)
                            dve.wait_ge(forget_ready.sem, forget_ready.at(layer, 1))
                            dve.tensor_copy(forget_b, spread(flat(forget[:, :, :]))).then_inc(forget_ready.sem, 1)
                        if (g, c) == (3, 3):
                            dve.wait_ge(cum_psum.sem, cum_psum.at(layer, 1))
                            dve.tensor_copy(flat(cum_q[:, :, :]), PS[:, 7, 0:NT * NH]).then_inc(cum_ready.sem, 1)
                        if (g, c) in ((4, 0), (4, 1)):
                            i = c
                            if i == 0:
                                dve.wait_ge(cum_ready.sem, cum_ready.at(layer, 1))
                            dve.wait_ge(score_psum.sem, score_psum.at(layer, i + 1))
                            width = (i + 1) * P
                            for h in range(NH):
                                src = PS[:, 5, h * P:(h + 1) * P] if i == 0 else PS[:, 6 + h // 2, (h % 2) * S:(h % 2 + 1) * S]
                                dve.scalar_tensor_tensor(probs[i][:, h, :], src, cum_q[:, i, h:h + 1], mask[:, S - width:S],
                                                         ALU.add, ALU.add).then_inc(score_ready.sem, 1)
                            cols = slice(i * NH, (i + 1) * NH)
                            dve.wait_ge(score_ready.sem, score_ready.at(layer, NH * (i + 1)))
                            dve.tensor_reduce(smax[:, cols], probs[i], AX.X, ALU.max).then_inc(max_step.sem, 1)
                            dve.wait_ge(max_step.sem, max_step.at(layer, 2 * i + 1))
                            dve.tensor_scalar(smax[:, cols], smax[:, cols], -1.0, None, ALU.mult).then_inc(max_step.sem, 1)
                        if (g, c) in ((4, 2), (4, 3)):
                            i = c - 2
                            cols = slice(i * NH, (i + 1) * NH)
                            dve.wait_ge(exp_ready.sem, exp_ready.at(layer, NH * (i + 1)))
                            dve.reciprocal(ssum[:, cols], ssum[:, cols]).then_inc(recip_ready.sem, 1)
                            dve.wait_ge(recip_ready.sem, recip_ready.at(layer, i + 1))
                            dve.tensor_tensor(probs[i], probs[i], spread(ssum[:, cols], NH, (i + 1) * P), ALU.mult)\
                               .then_inc(probs_ready.sem, 1)
                        if (g, c) == (5, 0):
                            for n in range(2):
                                ft_lo(layer, n + 1, PS[:, 5 + n, :].rearrange("p (h s) -> p h s", h=2), 8 + 2 * n)
                        if (g, c) == (5, 3):
                            dve.wait_ge(ret_psum.sem, ret_psum.at(layer, 1))
                            for n, bank in enumerate((4, 7)):
                                dve.tensor_tensor(ret_s[0][:, 2 * n:2 * n + 2, :],
                                                  PS[:, bank, :].rearrange("p (h l) -> p h l", h=2),
                                                  decay[:, 2 * n:2 * n + 2, :], ALU.mult).then_inc(ret_decayed.sem, 1)
                            dve.tensor_tensor(ret_s[1], PS[:, 5, :].rearrange("p (h l) -> p h l", h=NH), decay[:, :, 0:P],
                                              ALU.mult).then_inc(ret_decayed.sem, 1)
                        if (g, c) == (5, 7):
                            dve.wait_ge(y_psum.sem, y_psum.at(layer, 1))
                            head_norm(layer, 0, heads(banks(6)), heads(A5[:, 0:1024]))
                        if (g, c) == (6, 6):
                            for n in range(2):
                                dve.wait_ge(ret_turned.sem, ret_turned.at(layer, 1))
                                ft_lo(layer, n + 3, PS[:, 4 + n, :].rearrange("p (h s) -> p h s", h=2), 12 + 2 * n)
                        if (g, c) == (6, 7):
                            dve.wait_ge(in_read_s.sem, in_read_s.at(layer, 10))
                            head_norm(layer, 1, heads(A1[:, 0:1024]), heads(A1[:, 0:1024]))
                        if (g, c) == (7, 3):
                            dve.wait_ge(ws_turned.sem, ws_turned.at(layer, 1))
                            dve.tensor_tensor(wsT[:, :, :], PS[:, 4, :].rearrange("p (h t) -> p h t", h=NH),
                                              tri.unsqueeze(1).to_broadcast([P, NH, P]), ALU.mult).then_inc(ws_ready.sem, 1)
                        if (g, c) == (7, 7):
                            dve.wait_ge(chunk_used.sem, group_done(layer, GSU))
                            dve.tensor_tensor(uT, banks(IN_BANK[GSU]).rearrange("p (h s) -> p h s", h=NH), wide_rms,
                                              ALU.mult).then_inc(in_read_v.sem, 1)
                        if (g, c) == (8, 3):
                            dve.wait_ge(z_psum.sem, z_psum.at(layer, 1))
                            dve.tensor_tensor(zT.rearrange("p h (n t) -> p h n t", n=NT),
                                              banks(6).rearrange("p (h n t) -> p h n t", h=NH, n=NT),
                                              sbias[:, :, :].unsqueeze(2).to_broadcast([P, NH, NT, P]), ALU.add)\
                               .then_inc(z_step.sem, 1)
                            dve.wait_ge(z_step.sem, z_step.at(layer, 1))
                            dve.wait_ge(u_ready.sem, u_ready.at(layer, 1))
                            dve.tensor_tensor(flat(zT), flat(zT), flat(uT), ALU.mult).then_inc(z_step.sem, 1)
                            dve.wait_ge(z_step.sem, z_step.at(layer, 2))
                            for n in range(2):
                                ft_lo(layer, n + 5, zT[:, 2 * n:2 * n + 2, :], 4 + 2 * n)

                    splits(layer, g, steps, {False: in_width(g), True: in_width(g + 1)})

                def pool_steps(c):
                    if c == 2:
                        for w in range(4):
                            if w % 2 == 0:
                                dve.wait_ge(ft_hi.sem, ft_hi.at(layer, 7 + w // 2))
                            v = dve.scalar_tensor_tensor(FT[:, w, S:2 * S], PS[:, 4 + w // 2, (w % 2) * S:(w % 2 + 1) * S],
                                                         pscale[:, w:w + 1], f32(FT[:, w, 0:S]), ALU.mult, ALU.subtract)
                            if w % 2:
                                v.then_inc(ft_done.sem, 1)

                def mlp_rms(c):
                    if c == 5:
                        inverse_rms(layer, 1, 4)

                for gi in range(4):
                    splits(layer, NIN + gi, pool_steps if gi == 0 else None)
                    evacuate_down(layer, gi, gi % 2, 0, gi, 0, 8)
                for gi in range(4):
                    splits(layer, NIN + 4 + gi, mlp_rms if gi == 0 else None)
                    evacuate_up(layer, gi + 4, gi % 2, 0, gi)
                with dve.Fori(0, 3) as q:
                    with dve.Fori(0, 2) as i:
                        for s in range(2):
                            splits(layer, q * 8 + i * 2 + (NIN + 8 + s))
                            evacuate_down(layer, q * 8 + i * 2 + (8 + s), s, q + 1, i * 2 + s)
                    with dve.Fori(0, 2) as i:
                        for s in range(2):
                            splits(layer, q * 8 + i * 2 + (NIN + 12 + s))
                            evacuate_up(layer, q * 8 + i * 2 + (12 + s), s, q + 1, i * 2 + s)
                with dve.Fori(0, 2) as i:
                    for s in range(2):
                        splits(layer, i * 2 + (NIN + 32 + s))
                        evacuate_down(layer, i * 2 + (32 + s), s, 4, i * 2 + s, 1, 16)

            inverse_rms(DEPTH, 0, 2)
            rms_columns(DEPTH, 3)
            dve.wait_ge(col_ready.sem, col_ready.at(DEPTH, 1))
            for piece in range(1, 8, 2):
                n, g = divmod(piece, 4)
                dve.wait_ge(out_psum.sem, piece + 1)
                dve.tensor_scalar(out_sb[n][:, g * CW:(g + 1) * CW], PS[:, [6, 7, 0, 1, 4, 5, 6, 7][piece], :],
                                  rms_col[:, n:n + 1], None, ALU.mult).then_inc(out_v.sem, 1)

        @block.gpsimd
        def _(pool):
            def squares(layer, m, pair, first, tiles):
                if first:
                    pool.tensor_tensor(sq_acc[:, :, :], hT[:, tiles, :], hT[:, tiles, :], ALU.mult).then_inc(sq_step.sem, 2)
                else:
                    pool.tensor_tensor(sq[:, :, :], hT[:, tiles, :], hT[:, tiles, :], ALU.mult).then_inc(sq_step.sem, 1)
                    pool.wait_ge(sq_step.sem, sq_step.at(layer, pair * 2 + (16 * m + 1)))
                    pool.tensor_tensor(sq_acc[:, :, :], sq_acc[:, :, :], sq[:, :, :], ALU.add).then_inc(sq_step.sem, 1)
                pool.wait_ge(sq_step.sem, sq_step.at(layer, pair * 2 + (16 * m + 2)))

            def residual(layer, u, f, gi, q=None, norm=None, first=False):
                for p in range(2):
                    pool.wait_ge(combined.sem, combined.at(layer, u * 2 + (p + 1)))
                    tiles = ds(gi * 4 + 2 * p, 2)
                    if q is not None:
                        pool.wait_ge(rms_step.sem, rms_step.at(layer, 14))
                        pool.tensor_tensor(down[:, p, :, :], down[:, p, :, :],
                                           rms2[:, :].unsqueeze(1).to_broadcast([P, 2, S]), ALU.mult).then_inc(scaled.sem, 1)
                        pool.wait_ge(scaled.sem, scaled.at(layer, q * 8 + gi * 2 + (p + 1)))
                    pool.tensor_tensor(hT[:, tiles, :], hT[:, tiles, :], down[:, p, :, :], ALU.add).then_inc(h_done.sem, 1)
                if norm is not None:
                    for p in range(2):
                        pool.wait_ge(h_done.sem, h_done.at(layer, f * 8 + gi * 2 + (p + 1)))
                        squares(layer, norm, gi * 2 + p, first and p == 0, ds(gi * 4 + 2 * p, 2))

            for i in range(KT // 2):
                pool.wait_ge(hT_first.sem, i + 1)
                squares(0, 0, i, i == 0, slice(2 * i, 2 * i + 2))
            pool.sem_inc(sq_ready.sem, 1)
            pool.wait_ge(tab_in.sem, 16)

            with pool.Fori(0, DEPTH) as layer:
                pool.wait_ge(in_read_s.sem, in_read_s.at(layer, 2))
                x4 = qk.rearrange("p t (h e d) -> p t h e d", h=2 * NH, e=2)
                r4 = rot.rearrange("p t (h e d) -> p t h e d", h=2 * NH, e=2)
                t4 = rot_tmp.rearrange("p (t h d) -> p t h d", t=NT, h=2 * NH)
                cos, sin = rot_table(T_COS), rot_table(T_SIN)
                for e, (one, two, op) in enumerate(((cos, sin, ALU.subtract), (sin, cos, ALU.add))):
                    if e:
                        pool.wait_ge(rot_step.sem, rot_step.at(layer, 3))
                    pool.tensor_tensor(r4[:, :, :, e, :], x4[:, :, :, 0, :], one, ALU.mult).then_inc(rot_step.sem, 1)
                    pool.tensor_tensor(t4, x4[:, :, :, 1, :], two, ALU.mult).then_inc(rot_step.sem, 1)
                    pool.wait_ge(rot_step.sem, rot_step.at(layer, 3 * e + 2))
                    pool.tensor_tensor(r4[:, :, :, e, :], r4[:, :, :, e, :], t4, op).then_inc(rot_step.sem, 1)
                pool.wait_ge(in_read_s.sem, in_read_s.at(layer, 8))
                pool.wait_ge(small.sem, small.at(layer, 16 * 8))
                wide = lambda g: g[:, :].unsqueeze(1).to_broadcast([P, NT, GW])
                pool.tensor_tensor(swish, swish, wide(rgain), ALU.mult).then_inc(swish_gain.sem, 1)
                pool.wait_ge(swish_gain.sem, swish_gain.at(layer, 1))
                pool.wait_ge(norm_step.sem, norm_step.at(layer, 10))
                pool.tensor_tensor(y_ret, y_ret, swish, ALU.mult).then_inc(ret_out.sem, 1)
                pool.wait_ge(norm_step.sem, norm_step.at(layer, 20))
                pool.tensor_tensor(gv, gv, wide(sgain), ALU.mult).then_inc(sv_ready.sem, 1)

                for gi in range(4):
                    residual(layer, gi, 0, gi, norm=1, first=gi == 0)
                pool.sem_inc(sq_ready.sem, 1)
                with pool.Fori(0, 3) as q:
                    with pool.Fori(0, 4) as gi:
                        residual(layer, q * 8 + gi + 8, q + 1, gi, q=q)
                for gi in range(4):
                    residual(layer, 32 + gi, 4, gi, q=3, norm=2, first=gi == 0)
                pool.sem_inc(sq_ready.sem, 1)


def kernel(x, norm_mix_g, w_in, fox_b_f, pool_w, pool_scale, sgu_norm_g, sgu_w_s, sgu_b, ret_norm_g,
           w_out, norm_mlp_g, w_ff1, w_ff2, norm_final_g):
    import concourse.bacc as bacc
    from concourse.bass_utils import run_bass_kernel_spmd

    col = lambda g: np.asarray(g).reshape(KT, P).T
    after = [norm_mix_g[n] for n in range(1, DEPTH)] + [norm_final_g]
    arrays = {
        "x": np.asarray(x).reshape(S, D),
        "w_in": w_in, "w_out": w_out, "w_ff1": w_ff1, "w_ff2": w_ff2,
        "tables": constants(),
        "gain0": col(norm_mix_g[0]),
        "gains": np.stack([np.stack([col(norm_mlp_g[n]), col(after[n])], 1) for n in range(DEPTH)]),
        "fox_b": fox_b_f,
        "pool_w": np.asarray(pool_w).transpose(0, 2, 1, 3),
        "pool_scale": np.asarray(pool_scale).reshape(DEPTH, 4, P).transpose(0, 2, 1),
        "sgu_g": sgu_norm_g,
        "sgu_w": np.asarray(sgu_w_s).transpose(0, 2, 1, 3),
        "sgu_b": np.asarray(sgu_b).reshape(DEPTH, GW),
        "ret_g": ret_norm_g,
    }
    nc = bacc.Bacc("TRN2", target_bir_lowering=False, num_devices=1)
    ins, args = {}, []
    for name, a in arrays.items():
        a = np.ascontiguousarray(a)
        ins[f"in_{name}"] = a
        args.append(nc.dram_tensor(f"in_{name}", a.shape, mybir.dt.from_np(a.dtype), kind="ExternalInput").ap())
    args.append(nc.dram_tensor("out_h", (S, D), mybir.dt.float32, kind="ExternalOutput").ap())
    trunk(nc, *args)
    r = run_bass_kernel_spmd(nc, [ins], core_ids=[0])
    return r.results[0]["out_h"].reshape(1, S, D)
```

```python
import concourse.bass as bass
from concourse import mybir
from contextlib import ExitStack
import numpy as np

D = 2048
S = 256
DEPTH = 2
DFF = 4 * D
GW = D // 4
P = 128
NT = S // P
KT = D // P
NH = 4
HD = GW // NH
RQK = HD // 2
WINDOWS = (2, 4, 8, 16)
EPS = 1e-6
NEG_BIG = -1e30
Q_SCALE = HD ** -0.5
CW = 512
FCOLS = NH
CHUNKS = 8
CK = KT // CHUNKS
SLOTS = 4
LEAD = 3
W_IN = [(3 * GW, "T"), (4 * GW, "T"), (6 * GW, "N"), (5 * GW, "N"), (7 * GW + FCOLS, "N"),
        (8 * GW + FCOLS, "N"), (2 * GW, "N"), (GW, "T"), (0, "N")]
GQ, GK, GROT, GVF, GVR, GGR, GSV, GSU, GPOOL = range(9)
NIN = len(W_IN)
IN_BANK = [2, 0, 2, 0, 2, 0, 2, 0, 4]
OUT_BANK = [6, 7, 2, 3, 0, 1, 4, 6]
XT_BANK = [2, 3, 4, 5, 6, 7, 0, 1]
SETS = ((2, 3, 6, 7), (0, 1, 4, 5))
UD = 4 + 4 * 8
GROUPS = NIN + UD
NCH = GROUPS * CHUNKS
MIX_ORDER = [8, 9, 10, 11, 12, 13, 14, 15, 4, 5, 6, 7, 0, 1, 2, 3]
T_ID, T_ONE, T_EPS, T_TRI, T_NTRI, T_MASK, T_COS, T_SIN = 0, 128, 256, 260, 516, 772, 1028, 1092
T_DEC = 1156
T_BAND = T_DEC + NH * S
T_ALL = T_BAND + 4 * 3 * P
TAB_PIECES = [(T_TRI, T_DEC)] + [(at, at + 640) for at in range(T_DEC, T_ALL, 640)]


def constants():
    t = np.zeros((P, T_ALL), np.float32)
    i = np.arange(P)
    upper = (i[:, None] <= i[None, :]).astype(np.float32)
    t[:, T_ID:T_ID + P] = np.eye(P)
    t[:, T_ONE:T_ONE + P] = 1
    t[:, T_TRI:T_TRI + S] = np.concatenate([upper, np.ones((P, P))], 1)
    t[:, T_NTRI:T_NTRI + S] = -t[:, T_TRI:T_TRI + S]
    t[:, T_MASK + P:T_MASK + 2 * P] = np.where(upper.T > 0, 0, NEG_BIG)
    half = RQK // 2
    inv = np.exp(-(np.arange(half, dtype=np.float32) / half) * np.float32(np.log(10000.0))).astype(np.float32)
    ang = (np.arange(S, dtype=np.float32)[:, None] * inv).astype(np.float64)
    for n in range(NT):
        t[:, T_COS + n * half:T_COS + (n + 1) * half] = np.cos(ang[n * P:(n + 1) * P])
        t[:, T_SIN + n * half:T_SIN + (n + 1) * half] = np.sin(ang[n * P:(n + 1) * P])
    t[:, T_EPS] = EPS
    l = np.arange(S)
    for h in range(NH):
        gamma = 1.0 - 2.0 ** (-5.0 - h)
        d = l[None, :] - i[:, None]
        t[:, T_DEC + h * S:T_DEC + (h + 1) * S] = np.where(d >= 0, gamma ** np.maximum(d, 0), 0) * RQK ** -0.5
    for n, w in enumerate(WINDOWS):
        for b, (t0, s0) in enumerate(((0, 0), (0, P), (P, P))):
            tt, ss = t0 + i[:, None], s0 + i[None, :]
            inside = (tt <= ss) & (tt > ss - w)
            at = T_BAND + (n * 3 + b) * P
            t[:, at:at + P] = inside / np.minimum(ss + 1, w) - (tt == ss)
    return t


class Signal:

    def __init__(self, sem, per, credit=0):
        self.sem, self.per, self.credit = sem, per, credit

    def at(self, layer, k):
        return layer * self.per + (k + self.credit)


def trunk(nc, x, w_in, w_out, w_ff1, w_ff2, tables, gain0, gains, fox_b, pool_w, pool_scale,
          sgu_g, sgu_w, sgu_b, ret_g, out):
    F, R = mybir.dt.float32, mybir.dt.float32r
    ALU, ACT, AX = mybir.AluOpType, mybir.ActivationFunctionType, mybir.AxisListType
    ds = bass.ds

    by_chunk = lambda w: w.rearrange("l (c t p) n -> (l c) p t n", t=CK, p=P)
    w_in_v, w_out_v, ff1_v, ff2_v = by_chunk(w_in), by_chunk(w_out), by_chunk(w_ff1), by_chunk(w_ff2)

    ctx = ExitStack()
    with ctx:
        def sb(name, shape, dt=F):
            return ctx.enter_context(nc.sbuf_tensor(name, shape, dt))

        def sig(name, per=1, credit=0):
            return Signal(ctx.enter_context(nc.semaphore(name)), per, credit)

        stage = sb("stage", [P, SLOTS, CK, CW + FCOLS])
        w_hi = sb("w_hi", [P, SLOTS, CK, CW + FCOLS], R)
        w_lo = sb("w_lo", [P, SLOTS, CK, CW + FCOLS], R)
        XN = sb("XN", [P, KT, 2 * S], R)
        FT = sb("FT", [P, KT, 2 * S], R)
        hT = sb("hT", [P, KT, S])
        tab = sb("tab", [P, T_ALL])
        ident_r = sb("ident_r", [P, P], R)
        ntri_r = sb("ntri_r", [P, S], R)
        A1 = sb("A1", [P, 2048])
        A2 = sb("A2", [P, 2048])
        A3 = sb("A3", [P, 2048])
        A4 = sb("A4", [P, 6 * 256])
        A5 = sb("A5", [P, 6 * 256])
        v_fox = sb("v_fox", [P, NT, GW])
        A6 = sb("A6", [P, 1024])
        rms = sb("rms", [P, S])
        rms2 = sb("rms2", [P, S])
        sq_acc = sb("sq_acc", [P, 2, S])
        sq = sb("sq", [P, 2, S])
        mean, root = sq[:, 0, :], sq[:, 1, :]
        rms_col = sb("rms_col", [P, NT])
        gain = sb("gain", [P, 2, KT])
        fox_bias = sb("fox_bias", [P, NH])
        pscale = sb("pscale", [P, 4])
        pw = sb("pw", [P, 4, P])
        ws = sb("ws", [P, NH, P])
        wsT = sb("wsT", [P, NH, P])
        sbias = sb("sbias", [P, NH, P])
        sgain = sb("sgain", [P, GW])
        rgain = sb("rgain", [P, GW])
        forget = sb("forget", [P, NT, NH])
        f_abs = sb("f_abs", [P, NT, NH])
        f_min = sb("f_min", [P, NT, NH])
        cum_q = sb("cum_q", [P, NT, NH])
        smax = sb("smax", [P, NT * NH])
        ssum = sb("ssum", [P, NT * NH])
        hn = sb("hn", [P, 4, NT * NH])
        PS = ctx.enter_context(nc.psum_tensor("PS", [P, 8, 512], F))

        ident = tab[:, T_ID:T_ID + P]
        ones = tab[:, T_ONE:T_ONE + P]
        tri = tab[:, T_TRI:T_TRI + P]
        mask = tab[:, T_MASK:T_MASK + S]
        eps = tab[:, T_EPS:T_EPS + 1]
        half = RQK // 2
        rot_table = lambda at: tab[:, at:at + NT * half].rearrange("p (t d) -> p t d", t=NT)\
            .unsqueeze(2).to_broadcast([P, NT, 2 * NH, half])
        decay = tab[:, T_DEC:T_DEC + NH * S].rearrange("p (h l) -> p h l", h=NH)
        band = tab[:, T_BAND:T_ALL].rearrange("p (w b s) -> p w b s", w=4, b=3)

        x_nat = [A1, A2]
        tmp = A1[:, 0:1024].rearrange("p (a t s) -> p a t s", a=2, t=2)
        up = A1[:, 1024:2048].rearrange("p (a t s) -> p a t s", a=2, t=2)
        down = A2[:, 0:1024].rearrange("p (a t s) -> p a t s", a=2, t=2)
        sq_last = A1[:, 1024:2048].rearrange("p (t s) -> p t s", t=4)
        qT = A1[:, 0:1024].rearrange("p (h s) -> p h s", h=NH)
        kT = A1[:, 1024:2048].rearrange("p (h s) -> p h s", h=NH)
        gv = A1[:, 0:1024].rearrange("p (t n) -> p t n", t=NT)
        uT = A1[:, 1024:2048].rearrange("p (h s) -> p h s", h=NH)
        qk = A2[:, 0:1024].rearrange("p (t n) -> p t n", t=NT)
        rot = A2[:, 1024:2048].rearrange("p (t n) -> p t n", t=NT)
        swish = A2[:, 0:1024].rearrange("p (t n) -> p t n", t=NT)
        a_nat = A2[:, 1024:2048].rearrange("p (t n) -> p t n", t=NT)
        rot_tmp = A3[:, 0:512]
        rotT = A3[0:RQK, :].rearrange("p (h s) -> p h s", h=2 * NH)
        sq_head = A3[:, 0:1024]
        zT = A3[:, 0:1024].rearrange("p (h s) -> p h s", h=NH)
        pT = A3[:, 1024:2048].rearrange("p (w s) -> p w s", w=4)
        probs = (A4[:, 0:512].rearrange("p (h k) -> p h k", h=NH),
                 A4[:, 512:1536].rearrange("p (h k) -> p h k", h=NH))
        ret_s = (A4[:, 0:1024].rearrange("p (h l) -> p h l", h=NH),
                 A4[:, 1024:1536].rearrange("p (h l) -> p h l", h=NH))
        probsT = (A5[:, 0:1024].rearrange("p (h q) -> p h q", h=NH),
                  A5[:, 1024:1536].rearrange("p (h q) -> p h q", h=NH))
        y_ret = A5[:, 0:1024].rearrange("p (t n) -> p t n", t=NT)
        forget_b = [FT[:, 2 * n:2 * n + 2, :].rearrange("p a n -> p (a n)").rearrange("p (a n) -> p a n", a=NT * NH)
                    for n in range(2)]
        v_ret = A6[:, :].rearrange("p (t n) -> p t n", t=NT)
        out_sb = [A1, A2]

        f32 = lambda ap: ap.bitcast(F)
        flat = lambda ap: ap.rearrange("p a b -> p (a b)")

        def banks(b, n=2, parts=P):
            return PS[0:parts, b:b + n, :].rearrange("p b n -> p (b n)")

        staged = [sig(f"staged{n}", 16 * NCH // SLOTS) for n in range(SLOTS)]
        hi_done = sig("hi_done", NCH)
        lo_done = sig("lo_done", NCH, SLOTS)
        chunk_used = sig("chunk_used", NCH, SLOTS)
        half_done = sig("half_done", UD)
        tmp_ready = sig("tmp_ready", 2 * UD)
        combined = sig("combined", 2 * UD, 4)
        ff_ready = sig("ff_ready", 2 * 16)
        ft_hi = sig("ft_hi", 8 * 5)
        ft_done = sig("ft_done", 8 * 5)
        h_done = sig("h_done", 2 * 20, 2)
        sq_ready = sig("sq_ready", 1)
        sq_sum = sig("sq_sum", 4)
        sq_last_ready = sig("sq_last_ready", 2)
        res_step = sig("res_step", 2)
        sq_step = sig("sq_step", 12 + 16)
        scaled = sig("scaled", 2 * 15)
        xn_hi = sig("xn_hi", 16)
        xn_done = sig("xn_done", 16)
        sum_ready = sig("sum_ready", 2)
        root_ready = sig("root_ready", 2)
        rms_step = sig("rms_step", 2 * 7)
        rms_turned = sig("rms_turned", 1)
        col_ready = sig("col_ready", 1)
        in_read_v = sig("in_read_v", 3)
        in_read_s = sig("in_read_s", 12)
        small = sig("small", 16 * 8)
        gate_z = sig("gate_z", 4)
        gate_e = sig("gate_e", 2)
        forget_ready = sig("forget_ready", 2)
        cum_psum = sig("cum_psum", 1)
        cum_ready = sig("cum_ready", 1)
        rot_step = sig("rot_step", 6)
        rot_turned = sig("rot_turned", 1)
        rot_ready = sig("rot_ready", 2)
        score_psum = sig("score_psum", 2)
        score_ready = sig("score_ready", 8)
        max_step = sig("max_step", 4)
        exp_ready = sig("exp_ready", 8)
        recip_ready = sig("recip_ready", 2)
        probs_ready = sig("probs_ready", 2)
        probs_turned = sig("probs_turned", 3)
        probsT_ready = sig("probsT_ready", 3)
        fox_psum = sig("fox_psum", 1)
        ret_psum = sig("ret_psum", 1)
        ret_decayed = sig("ret_decayed", 3)
        y_psum = sig("y_psum", 1)
        norm_step = sig("norm_step", 2 * 10)
        norm_sq = sig("norm_sq", 2)
        norm_root = sig("norm_root", 2)
        swish_gain = sig("swish_gain", 1)
        ret_out = sig("ret_out", 1)
        ret_turned = sig("ret_turned", 1)
        ws_turned = sig("ws_turned", 1)
        ws_ready = sig("ws_ready", 1)
        sv_ready = sig("sv_ready", 1)
        u_ready = sig("u_ready", 1)
        z_psum = sig("z_psum", 1)
        z_step = sig("z_step", 2)
        pool_psum = sig("pool_psum", 1)
        pT_ready = sig("pT_ready", 1)
        poolw_psum = sig("poolw_psum", 1)
        x_in = [sig(f"x_in{n}", 0) for n in range(4)]
        ident_in = sig("ident_in", 0)
        tab_in = sig("tab_in", 0)
        gain0_in = sig("gain0_in", 0)
        xT_psum = sig("xT_psum", 0)
        hT_first = sig("hT_first", 0)
        exact_r = sig("exact_r", 0)
        forget_hi = sig("forget_hi", 1)
        out_psum = sig("out_psum", 0)
        out_s = sig("out_s", 0)
        out_v = sig("out_v", 0)
        load_turn = sig("load_turn", 0)
        turn_start = sig("turn_start", 0)
        stored = sig("stored", 0)

        def group_done(layer, g):
            return chunk_used.at(layer, g * CHUNKS + CHUNKS)

        block = ctx.enter_context(nc.Block())

        def in_width(g):
            return CW + FCOLS if g == GROT else CW

        @block.sync
        def _(sp):
            def load_chunk(layer, g, c, src):
                sp.wait_ge(lo_done.sem, lo_done.at(layer, g * CHUNKS + (c + 1 - SLOTS)))
                sp.sem_inc(load_turn.sem, 1)
                width = src.shape[-1]
                sp.dma_start(stage[:, c % SLOTS, :, 0:width], src).then_inc(staged[c % SLOTS].sem, 16)

            def load_up(layer, q, gi):
                for c in range(CHUNKS):
                    load_chunk(layer, NIN + 4 + q * 8 + gi, c,
                               ff1_v[layer * CHUNKS + c, :, :, ds(q * D + gi * CW, CW)])

            def load_down(layer, q, gi):
                for c in range(CHUNKS):
                    load_chunk(layer, NIN + 8 + q * 8 + gi, c,
                               ff2_v[layer * (4 * CHUNKS) + q * CHUNKS + c, :, :, ds(gi * CW, CW)])

            sp.dma_start(tab[:, 0:T_TRI], tables[:, 0:T_TRI]).then_inc(ident_in.sem, 16)
            sp.dma_start(gain[:, 1, :], gain0).then_inc(gain0_in.sem, 16)
            sp.wait_ge(x_in[0].sem, 16 * NT)
            with sp.Fori(0, DEPTH) as layer:
                for g, (col, _) in enumerate(W_IN):
                    for c in range(CHUNKS):
                        load_chunk(layer, g, c, w_in_v[layer * CHUNKS + c, :, :, col:col + in_width(g)])
                    if g == GK:
                        sp.dma_start(gain[:, :, :], gains[layer]).then_inc(small.sem, 16)
                        sp.dma_start(fox_bias[:, :], fox_b[ds(layer, 1), :].to_broadcast([P, NH])).then_inc(small.sem, 16)
                        sp.dma_start(pscale[:, :], pool_scale[layer]).then_inc(small.sem, 16)
                        sp.dma_start(pw[:, :, :], pool_w[layer]).then_inc(small.sem, 16)
                        sp.dma_start(ws[:, :, :], sgu_w[layer]).then_inc(small.sem, 16)
                        sp.dma_start(flat(sbias[:, :, :]), sgu_b[ds(layer, 1), :].to_broadcast([P, GW])).then_inc(small.sem, 16)
                        sp.dma_start(sgain[:, :], sgu_g[ds(layer, 1), :].to_broadcast([P, GW])).then_inc(small.sem, 16)
                        sp.dma_start(rgain[:, :], ret_g[ds(layer, 1), :].to_broadcast([P, GW])).then_inc(small.sem, 16)
                with sp.Fori(0, 4) as gi:
                    for c in range(CHUNKS):
                        load_chunk(layer, gi + NIN, c,
                                   w_out_v[layer * CHUNKS + MIX_ORDER[CK * c] // CK, :, :, ds(gi * CW, CW)])
                with sp.Fori(0, 4) as q:
                    with sp.Fori(0, 4) as gi:
                        load_up(layer, q, gi)
                    with sp.Fori(0, 4) as gi:
                        load_down(layer, q, gi)
            for c in range(LEAD):
                load_chunk(DEPTH, 0, c, w_in_v[c, :, :, W_IN[0][0]:W_IN[0][0] + CW])
            for n in range(4):
                for t in range(NT):
                    piece = NT * n + t
                    sp.wait_ge([out_s, out_v][piece % 2].sem, piece // 2 + 1)
                    sp.dma_start(out[t * P:(t + 1) * P, n * CW:(n + 1) * CW],
                                 out_sb[t][:, n * CW:(n + 1) * CW]).then_inc(stored.sem, 16)
            sp.wait_ge(stored.sem, 16 * 4 * NT)

        @block.tensor
        def _(pe):
            def chunk_ready(layer, g, c):
                pe.wait_ge(lo_done.sem, lo_done.at(layer, g * CHUNKS + (c + 1)))

            def wide_group(layer, u, parity, moving, ready, ready_at, order, at_chunk=None):
                for c in range(CHUNKS):
                    chunk_ready(layer, u + NIN, c)
                    pe.wait_ge(ready.sem, ready.at(layer, ready_at + (c + 1)))
                    for t in range(CK):
                        kt = order[CK * c + t]
                        first, last = c == 0 and t == 0, c == CHUNKS - 1 and t == CK - 1
                        for j in range(4):
                            if first and j % 2 == 0:
                                pe.wait_ge(combined.sem, combined.at(layer, u * 2 + (j // 2 + 1 - 4)))
                            bank = SETS[parity][j]
                            cols = slice(j * P, (j + 1) * P)
                            both = lambda start, stop, skip: pe.matmul(
                                PS[:, bank, :], w_hi[:, c % SLOTS, t, cols], moving[:, kt, :],
                                start=start, stop=stop, skip_group_check=skip)
                            small_part = lambda: pe.matmul(
                                PS[:, bank, 0:S], w_lo[:, c % SLOTS, t, cols], moving[:, kt, 0:S],
                                start=False, stop=False, skip_group_check=True)
                            if last:
                                small_part()
                                mm = both(False, True, False)
                                if j == 1:
                                    mm.then_inc(half_done.sem, 1)
                            else:
                                both(first, False, False)
                                mm = small_part()
                            if j == 3 and t == CK - 1:
                                mm.then_inc(chunk_used.sem, 1)
                    if at_chunk:
                        at_chunk(c)

            def narrow_T(layer, g, c):
                for t in range(CK):
                    kt = CK * c + t
                    for j in range(4):
                        bank, at = IN_BANK[g] + j // 2, (j % 2) * S
                        cols = slice(j * P, (j + 1) * P)
                        first, last = kt == 0, kt == KT - 1
                        dst = PS[:, bank, at:at + S]
                        pe.matmul(dst, w_hi[:, c % SLOTS, t, cols], XN[:, kt, 0:S],
                                  start=first and j % 2 == 0, stop=False, skip_group_check=True)
                        pe.matmul(dst, w_hi[:, c % SLOTS, t, cols], XN[:, kt, S:2 * S],
                                  start=False, stop=False, skip_group_check=True)
                        mm = pe.matmul(dst, w_lo[:, c % SLOTS, t, cols], XN[:, kt, 0:S],
                                       start=False, stop=last, skip_group_check=True)
                return mm

            def narrow_N(layer, g, c):
                for t in range(CK):
                    kt = CK * c + t
                    for n in range(NT):
                        x_hi = XN[:, kt, n * P:(n + 1) * P]
                        x_lo = XN[:, kt, S + n * P:S + (n + 1) * P]
                        if g == GROT:
                            jobs = [(PS[:, 6 + n, 0:FCOLS + S], slice(0, FCOLS + S)),
                                    (PS[:, IN_BANK[g] + n, 0:S], slice(FCOLS + S, FCOLS + CW))]
                        else:
                            jobs = [(PS[:, IN_BANK[g] + n, :], slice(0, CW))]
                        for dst, cols in jobs:
                            hi, lo = w_hi[:, c % SLOTS, t, cols], w_lo[:, c % SLOTS, t, cols]
                            pe.matmul(dst, x_hi, hi, start=kt == 0, stop=False)
                            pe.matmul(dst, x_hi, lo, start=False, stop=False)
                            mm = pe.matmul(dst, x_lo, hi, start=False, stop=kt == KT - 1)
                return mm

            def sum_squares(bank, layer, m):
                pe.wait_ge(sq_sum.sem, sq_sum.at(layer, m + 3))
                pe.matmul(PS[:, bank, 0:S], ones, sq_acc[:, 0, :], start=True, stop=True).then_inc(sum_ready.sem, 1)

            def turn_rms(bank, layer, k):
                pe.wait_ge(rms_step.sem, rms_step.at(layer, k))
                for n in range(NT):
                    mm = pe.matmul(PS[:, bank, n:n + 1], rms[0:1, n * P:(n + 1) * P], ones[0:1, 0:1],
                                   start=True, stop=True)
                mm.then_inc(rms_turned.sem, 1)

            def turn(dst, src):
                return pe.matmul(dst, src, ident, start=True, stop=True, is_transpose=True)

            def running_sums(layer):
                pe.wait_ge(tab_in.sem, 16 * len(TAB_PIECES))
                pe.wait_ge(forget_ready.sem, forget_ready.at(layer, 1))
                pe.matmul(PS[:, 7, 0:NH], tri, forget[:, 0, :], start=True, stop=True)
                pe.matmul(PS[:, 7, NH:2 * NH], ones, forget[:, 0, :], start=True, stop=False)
                pe.matmul(PS[:, 7, NH:2 * NH], tri, forget[:, 1, :], start=False, stop=True).then_inc(cum_psum.sem, 1)

            def turn_rotated(layer):
                pe.wait_ge(rot_step.sem, rot_step.at(layer, 6))
                pe.wait_ge(cum_ready.sem, cum_ready.at(layer, 1))
                pe.sem_inc(turn_start.sem, 1)
                for h in range(2 * NH):
                    for n in range(NT):
                        at = (2 * (h % 2) + n) * P
                        mm = turn(PS[0:RQK, 4 + h // 2, at:at + P], rot[:, n, h * RQK:(h + 1) * RQK])
                mm.then_inc(rot_turned.sem, 1)

            def fox_scores(layer, i):
                pe.wait_ge(forget_ready.sem, forget_ready.at(layer, 2))
                pe.wait_ge(in_read_v.sem, in_read_v.at(layer, 2))
                pe.wait_ge(rot_ready.sem, rot_ready.at(layer, 2))
                pe.wait_ge(exact_r.sem, 2)
                for h in range(NH):
                    q = qT[:, h, i * P:(i + 1) * P]
                    if i == 0:
                        dst = PS[:, 5, h * P:(h + 1) * P]
                        pe.matmul(dst, q, kT[:, h, 0:P], start=True, stop=False)
                        for n in range(2):
                            mm = pe.matmul(dst, forget_b[n][:, h, :], ntri_r[:, 0:P], start=False, stop=n == 1)
                    else:
                        bank, at = 6 + h // 2, (h % 2) * S
                        pe.matmul(PS[:, bank, at:at + S], q, kT[:, h, :], start=True, stop=False)
                        for n in range(2):
                            pe.matmul(PS[:, bank, at + P:at + S], forget_b[n][:, NH + h, :], ntri_r[:, 0:P],
                                      start=False, stop=False, skip_group_check=True)
                        for n in range(2):
                            mm = pe.matmul(PS[:, bank, at:at + S], forget_b[n][:, h, :], ntri_r[:, :],
                                           start=False, stop=n == 1)
                mm.then_inc(score_psum.sem, 1)

            def turn_probs(layer):
                for n, (bank, i, k) in enumerate(((5, 0, 0), (6, 1, 0), (7, 1, 1))):
                    pe.wait_ge(probs_ready.sem, probs_ready.at(layer, i + 1))
                    for h in range(NH):
                        mm = turn(PS[:, bank, h * P:(h + 1) * P], probs[i][:, h, k * P:(k + 1) * P])
                    mm.then_inc(probs_turned.sem, 1)

            def fox_output(layer):
                pe.wait_ge(probsT_ready.sem, probsT_ready.at(layer, 3))
                pe.wait_ge(in_read_s.sem, in_read_s.at(layer, 4))
                for h in range(NH):
                    bank, at = 5 + h // 2, (h % 2) * S
                    v0, v1 = (v_fox[:, n, h * HD:(h + 1) * HD] for n in range(NT))
                    pe.matmul(PS[:, bank, at:at + P], v0, probsT[0][:, h, 0:P], start=True, stop=True)
                    pe.matmul(PS[:, bank, at + P:at + S], v0, probsT[0][:, h, P:S], start=True, stop=False)
                    mm = pe.matmul(PS[:, bank, at + P:at + S], v1, probsT[1][:, h, :], start=False, stop=True)
                mm.then_inc(fox_psum.sem, 1)

            def ret_scores(layer):
                pe.wait_ge(ft_done.sem, ft_done.at(layer, 2))
                for h in range(NH):
                    q, k = rotT[:, h, :], rotT[:, NH + h, :]
                    bank, at = 4 if h < 2 else 7, (h % 2) * S
                    pe.matmul(PS[:, bank, at:at + S], k[:, 0:P], q, start=True, stop=True)
                for h in range(NH):
                    q, k = rotT[:, h, :], rotT[:, NH + h, :]
                    mm = pe.matmul(PS[:, 5, h * P:(h + 1) * P], k[:, P:S], q[:, P:S], start=True, stop=True)
                mm.then_inc(ret_psum.sem, 1)

            def ret_output(layer):
                pe.wait_ge(ret_decayed.sem, ret_decayed.at(layer, 3))
                pe.wait_ge(in_read_s.sem, in_read_s.at(layer, 6))
                for h in range(NH):
                    v0, v1 = (v_ret[:, n, h * HD:(h + 1) * HD] for n in range(NT))
                    cols = slice(h * P, (h + 1) * P)
                    pe.matmul(PS[:, 6, cols], ret_s[0][:, h, 0:P], v0, start=True, stop=True)
                    pe.matmul(PS[:, 7, cols], ret_s[0][:, h, P:S], v0, start=True, stop=False)
                    mm = pe.matmul(PS[:, 7, cols], ret_s[1][:, h, :], v1, start=False, stop=True)
                mm.then_inc(y_psum.sem, 1)

            def turn_ret(layer):
                pe.wait_ge(ret_out.sem, ret_out.at(layer, 1))
                for h in range(NH):
                    for n in range(NT):
                        at = (h % 2) * S + n * P
                        mm = turn(PS[:, 4 + h // 2, at:at + P], y_ret[:, n, h * HD:(h + 1) * HD])
                mm.then_inc(ret_turned.sem, 1)

            def turn_ws(layer):
                pe.wait_ge(small.sem, small.at(layer, 16 * 8))
                pe.wait_ge(ft_done.sem, ft_done.at(layer, 4))
                for h in range(NH):
                    mm = turn(PS[:, 4, h * P:(h + 1) * P], ws[:, h, :])
                mm.then_inc(ws_turned.sem, 1)

            def mix_positions(layer):
                pe.wait_ge(sv_ready.sem, sv_ready.at(layer, 1))
                pe.wait_ge(ws_ready.sem, ws_ready.at(layer, 1))
                for h in range(NH):
                    for n in range(NT):
                        at = (h % 2) * S + n * P
                        mm = pe.matmul(PS[:, 6 + h // 2, at:at + P], gv[:, n, h * HD:(h + 1) * HD], wsT[:, h, :],
                                       start=True, stop=True)
                mm.then_inc(z_psum.sem, 1)

            def pool_means(layer):
                pe.wait_ge(in_read_s.sem, in_read_s.at(layer, 12))
                for w in range(4):
                    bank, at = w // 2, (w % 2) * S
                    a0, a1 = (a_nat[:, n, w * P:(w + 1) * P] for n in range(NT))
                    pe.matmul(PS[:, bank, at:at + P], a0, band[:, w, 0, :], start=True, stop=True)
                    pe.matmul(PS[:, bank, at + P:at + S], a0, band[:, w, 1, :], start=True, stop=False)
                    mm = pe.matmul(PS[:, bank, at + P:at + S], a1, band[:, w, 2, :], start=False, stop=True)
                mm.then_inc(pool_psum.sem, 1)

            def pool_product(layer):
                pe.wait_ge(pT_ready.sem, pT_ready.at(layer, 1))
                for w in range(4):
                    mm = pe.matmul(PS[:, 4 + w // 2, (w % 2) * S:(w % 2 + 1) * S], pw[:, w, :], pT[:, w, :],
                                   start=True, stop=True)
                mm.then_inc(poolw_psum.sem, 1)

            def pair_loop():
                return nc.Fori(0, 2, engines=[mybir.EngineType.PE], hint_back_edge=True)

            pe.wait_ge(ident_in.sem, 16)
            for i in range(KT // 2):
                if i % 2 == 0:
                    pe.wait_ge(x_in[i // 2].sem, 16 * NT)
                for t in range(2):
                    for n in range(NT):
                        at = (2 * t + n) * P
                        mm = turn(PS[:, XT_BANK[i], at:at + P], x_nat[n][:, (2 * i + t) * P:(2 * i + t + 1) * P])
                mm.then_inc(xT_psum.sem, 1)
            pe.wait_ge(hT_first.sem, 2)

            with pe.Fori(0, DEPTH) as layer:
                for g in range(NIN):
                    for c in range(CHUNKS):
                        chunk_ready(layer, g, c)
                        if g == 0:
                            pe.wait_ge(xn_done.sem, xn_done.at(layer, c + 1))
                        if c == 0:
                            if g == 0:
                                pe.wait_ge(combined.sem, combined.at(layer, -2))
                            if g == 1:
                                pe.wait_ge(combined.sem, combined.at(layer, 0))
                            if g == GROT:
                                pe.wait_ge(in_read_v.sem, in_read_v.at(layer, 1))
                            if g == GVF:
                                pe.wait_ge(in_read_v.sem, in_read_v.at(layer, 2))
                            if GVR <= g <= GSU:
                                pe.wait_ge(in_read_s.sem, in_read_s.at(layer, 2 * (g - 3)))
                            if g == GPOOL:
                                pe.wait_ge(ws_ready.sem, ws_ready.at(layer, 1))
                        mm = (narrow_T if W_IN[g][1] == "T" else narrow_N)(layer, g, c)
                        mm.then_inc(chunk_used.sem, 1)
                        if (g, c) == (0, 6):
                            sum_squares(4, layer, 0)
                        if (g, c) == (1, 1):
                            turn_rms(5, layer, 6)
                        if (g, c) == (3, 3):
                            running_sums(layer)
                        if (g, c) == (3, 6):
                            turn_rotated(layer)
                        if (g, c) == (4, 0):
                            fox_scores(layer, 0)
                        if (g, c) == (4, 1):
                            fox_scores(layer, 1)
                        if (g, c) == (4, 5):
                            turn_probs(layer)
                        if (g, c) == (5, 0):
                            fox_output(layer)
                        if (g, c) == (5, 3):
                            ret_scores(layer)
                        if (g, c) == (5, 6):
                            ret_output(layer)
                        if (g, c) == (6, 6):
                            turn_ret(layer)
                        if (g, c) == (7, 3):
                            turn_ws(layer)
                        if (g, c) == (8, 3):
                            mix_positions(layer)

                def pool_steps(c):
                    if c == 0:
                        pool_means(layer)
                    if c == 2:
                        pool_product(layer)

                natural = list(range(KT))
                for gi in range(4):
                    if gi == 0:
                        pe.wait_ge(z_step.sem, z_step.at(layer, 1))
                    wide_group(layer, gi, gi % 2, FT, ft_done, 0, MIX_ORDER, pool_steps if gi == 0 else None)

                def mlp_sum(c):
                    if c == 5:
                        sum_squares(4, layer, 1)

                for gi in range(4):
                    if gi == 1:
                        pe.wait_ge(rms_step.sem, rms_step.at(layer, 6 + 7))
                    wide_group(layer, gi + 4, gi % 2, XN, xn_done, 8, natural, mlp_sum if gi == 0 else None)
                with pe.Fori(0, 3) as q:
                    with pair_loop() as i:
                        for s in range(2):
                            wide_group(layer, q * 8 + i * 2 + (8 + s), s, FT, ft_done, q * 8 + 8, natural)
                    with pair_loop() as i:
                        for s in range(2):
                            wide_group(layer, q * 8 + i * 2 + (12 + s), s, XN, xn_done, 8, natural)
                with pair_loop() as i:
                    for s in range(2):
                        wide_group(layer, i * 2 + (32 + s), s, FT, ft_done, 32, natural)

            def out_piece(piece):
                g, n = divmod(piece, NT)
                for j in range(4):
                    dst = PS[:, OUT_BANK[piece], j * P:(j + 1) * P]
                    pe.matmul(dst, XN[:, 4 * g + j, n * P:(n + 1) * P], ident_r[:, :], start=True, stop=False)
                    mm = pe.matmul(dst, XN[:, 4 * g + j, S + n * P:S + (n + 1) * P], ident_r[:, :],
                                   start=False, stop=True)
                mm.then_inc(out_psum.sem, 1)

            pe.wait_ge(xn_done.sem, xn_done.at(DEPTH, 6))
            for piece in range(3):
                out_piece(piece)

            def column_sums(parts, first=False, last=False):
                for n, part in enumerate(parts):
                    for t in range(NT):
                        mm = pe.matmul(PS[:, 5, t:t + 1], part[:, t * P:(t + 1) * P], ones[:, 0:1],
                                       start=first and n == t == 0, stop=last and n == len(parts) - 1,
                                       skip_group_check=True)
                return mm

            pe.wait_ge(combined.sem, combined.at(DEPTH, 0))
            pe.wait_ge(sq_ready.sem, sq_ready.at(DEPTH, 0))
            column_sums([sq_acc[:, n, :] for n in range(2)], first=True)
            pe.wait_ge(sq_last_ready.sem, sq_last_ready.at(DEPTH, 1))
            column_sums([sq_last[:, n, :] for n in range(2)])
            out_piece(3)
            pe.wait_ge(sq_last_ready.sem, sq_last_ready.at(DEPTH, 2))
            column_sums([sq_last[:, n, :] for n in range(2, 4)], last=True).then_inc(sum_ready.sem, 1)
            out_piece(4)
            out_piece(5)
            pe.wait_ge(xn_done.sem, xn_done.at(DEPTH, 8))
            out_piece(6)
            pe.wait_ge(out_s.sem, 1)
            out_piece(7)

        @block.scalar
        def _(act):
            def split_hi(layer, g, k, width=CW):
                slot = k % SLOTS
                act.wait_ge(staged[slot].sem, staged[slot].at(layer, g * 32 + (k // SLOTS + 1) * 16))
                act.wait_ge(chunk_used.sem, chunk_used.at(layer, g * CHUNKS + (k + 1 - SLOTS)))
                act.activation(w_hi[:, slot, :, 0:width], stage[:, slot, :, 0:width], ACT.Copy).then_inc(hi_done.sem, 1)

            def splits(layer, g, at_chunk=None, widths=None):
                for c in range(CHUNKS):
                    split_hi(layer, g, c + LEAD, (widths or {}).get(c + LEAD >= CHUNKS, CW))
                    if at_chunk:
                        at_chunk(c)

            def read_tmp(layer, u, parity, p):
                if p == 0:
                    act.wait_ge(half_done.sem, half_done.at(layer, u + 1))
                else:
                    act.wait_ge(chunk_used.sem, group_done(layer, u + NIN))
                act.wait_ge(combined.sem, combined.at(layer, u * 2 + (p - 1)))
                b = SETS[parity][2 * p]
                act.activation(tmp[:, p, :, :], PS[:, b:b + 2, S:2 * S], ACT.Copy).then_inc(tmp_ready.sem, 1)

            def evacuate_up(layer, u, parity, q, gi):
                for p in range(2):
                    read_tmp(layer, u, parity, p)
                for p in range(2):
                    act.wait_ge(ff_ready.sem, ff_ready.at(layer, q * 8 + gi * 2 + (p + 1)))
                    act.activation(FT[:, ds(gi * 4 + 2 * p, 2), 0:S], up[:, p, :, :], ACT.Copy).then_inc(ft_hi.sem, 1)

            def norm_hi(g_cols, tile0):
                for t in range(2):
                    a = act.activation(XN[:, ds(tile0 + t, 1), 0:S].rearrange("p o s -> p (o s)"),
                                       hT[:, ds(tile0 + t, 1), :].rearrange("p o s -> p (o s)"), ACT.Copy,
                                       scale=g_cols[:, ds(tile0 + t, 1)])
                a.then_inc(xn_hi.sem, 1)

            def evacuate_down(layer, u, parity):
                for p in range(2):
                    read_tmp(layer, u, parity, p)

            def group_hi(layer, f, gi, gain_row):
                for p in range(2):
                    act.wait_ge(h_done.sem, h_done.at(layer, f * 8 + gi * 2 + (p + 1)))
                    norm_hi(gain[:, gain_row, :], gi * 4 + 2 * p)

            def last_hi(layer):
                group_hi(layer, -1, 3, 1)

            def last_squares(layer):
                for p in range(2):
                    act.wait_ge(h_done.sem, h_done.at(layer, p - 1))
                    act.activation(sq_last[:, 2 * p:2 * p + 2, :], hT[:, 12 + 2 * p:14 + 2 * p, :], ACT.Square)\
                       .then_inc(sq_last_ready.sem, 1)

            def root_of_mean(layer, m, bank):
                act.wait_ge(sum_ready.sem, sum_ready.at(layer, m + 1))
                act.activation(root, PS[:, bank, 0:S], ACT.Sqrt, scale=1.0 / D, bias=eps).then_inc(root_ready.sem, 1)

            def read_natural(layer, g, dst, func):
                act.wait_ge(chunk_used.sem, group_done(layer, g))
                for n in range(NT):
                    act.activation(dst[:, n, :], PS[:, IN_BANK[g] + n, :], func, scale=rms_col[:, n:n + 1])\
                       .then_inc(in_read_s.sem, 1)

            def head_squares(layer, k, src):
                act.wait_ge(norm_step.sem, norm_step.at(layer, 10 * k + 3))
                act.activation(sq_head, src.rearrange("p t n -> p (t n)"), ACT.Square).then_inc(norm_sq.sem, 1)

            def head_root(layer, k):
                act.wait_ge(norm_step.sem, norm_step.at(layer, 10 * k + 4))
                act.activation(hn[:, 1, :], hn[:, 0, :], ACT.Sqrt, scale=1.0 / HD, bias=eps).then_inc(norm_root.sem, 1)

            def ft_hi_from(src, tile0):
                act.activation(FT[:, tile0:tile0 + 2, 0:S], src, ACT.Copy).then_inc(ft_hi.sem, 1)

            for k in range(4):
                if k == 3:
                    act.wait_ge(x_in[0].sem, 16 * NT)
                for n in range(NT):
                    act.dma_start(x_nat[n][:, k * CW:(k + 1) * CW], x[n * P:(n + 1) * P, k * CW:(k + 1) * CW])\
                       .then_inc(x_in[k].sem, 16)
            act.wait_ge(ident_in.sem, 16)
            act.activation(ident_r[:, :], ident, ACT.Copy).then_inc(exact_r.sem, 1)
            act.wait_ge(gain0_in.sem, 16)
            for i in range(6):
                act.wait_ge(hT_first.sem, i + 1)
                norm_hi(gain[:, 1, :], 2 * i)
                if i in (2, 3, 5):
                    split_hi(0, 0, (2, 3, 5).index(i))

            with act.Fori(0, DEPTH) as layer:
                for g in range(NIN):
                    def steps(c):
                        if (g, c) == (0, 3):
                            act.wait_ge(hT_first.sem, KT // 2)
                            last_hi(layer)
                        if (g, c) == (0, 4):
                            last_squares(layer)
                        if (g, c) == (0, 6):
                            root_of_mean(layer, 0, 4)
                        if (g, c) == (1, 2):
                            act.wait_ge(tab_in.sem, 16 * len(TAB_PIECES))
                            act.activation(ntri_r[:, :], tab[:, T_NTRI:T_NTRI + S], ACT.Copy).then_inc(exact_r.sem, 1)
                        if (g, c) == (2, 7):
                            act.wait_ge(col_ready.sem, col_ready.at(layer, 1))
                            act.wait_ge(small.sem, small.at(layer, 16 * 8))
                            act.wait_ge(gate_z.sem, gate_z.at(layer, 2))
                            for n in range(NT):
                                for k, src in enumerate((PS[:, 6 + n, FCOLS:FCOLS + S], PS[:, IN_BANK[GROT] + n, 0:S])):
                                    a = act.activation(qk[:, n, k * S:(k + 1) * S], src, ACT.Copy, scale=rms_col[:, n:n + 1])
                                a.then_inc(in_read_s.sem, 1)
                        if (g, c) == (3, 0):
                            act.wait_ge(gate_z.sem, gate_z.at(layer, 3))
                            act.activation(f_abs[:, :, :], f_abs[:, :, :], ACT.Exp, scale=-1.0).then_inc(gate_e.sem, 1)
                            act.wait_ge(gate_e.sem, gate_e.at(layer, 1))
                            act.activation(f_abs[:, :, :], f_abs[:, :, :], ACT.Ln, bias=1.0).then_inc(gate_e.sem, 1)
                        if (g, c) == (3, 1):
                            act.wait_ge(forget_ready.sem, forget_ready.at(layer, 1))
                            act.activation(forget_b[0], flat(forget[:, :, :]).unsqueeze(2).to_broadcast([P, NT * NH, P]),
                                           ACT.Copy).then_inc(forget_hi.sem, 1)
                        if (g, c) == (3, 6):
                            act.wait_ge(rot_turned.sem, rot_turned.at(layer, 1))
                            for n in range(2):
                                act.activation(flat(rotT[:, 4 * n:4 * n + 4, :]), banks(4 + 2 * n, 2, RQK), ACT.Copy)\
                                   .then_inc(rot_ready.sem, 1)
                        if (g, c) == (3, 7):
                            read_natural(layer, GVF, v_fox, ACT.Copy)
                        if (g, c) in ((4, 1), (4, 2)):
                            i = c - 1
                            act.wait_ge(max_step.sem, max_step.at(layer, 2 * i + 2))
                            for h in range(NH):
                                k = i * NH + h
                                act.activation(probs[i][:, h, :], probs[i][:, h, :], ACT.Exp, bias=smax[:, k:k + 1],
                                               accum_out=ssum[:, k:k + 1]).then_inc(exp_ready.sem, 1)
                        if (g, c) == (4, 5):
                            for n, dst in enumerate((probsT[0][:, :, 0:P], probsT[0][:, :, P:S], probsT[1])):
                                act.wait_ge(probs_turned.sem, probs_turned.at(layer, n + 1))
                                act.activation(dst, PS[:, 5 + n, :].rearrange("p (h q) -> p h q", h=NH), ACT.Copy)\
                                   .then_inc(probsT_ready.sem, 1)
                        if (g, c) == (4, 7):
                            read_natural(layer, GVR, v_ret, ACT.Copy)
                        if (g, c) == (5, 0):
                            act.wait_ge(fox_psum.sem, fox_psum.at(layer, 1))
                            for n in range(2):
                                ft_hi_from(PS[:, 5 + n, :].rearrange("p (h s) -> p h s", h=2), 8 + 2 * n)
                        if (g, c) == (5, 7):
                            read_natural(layer, GGR, swish, ACT.Silu)
                        if (g, c) == (6, 0):
                            head_squares(layer, 0, y_ret)
                        if (g, c) == (6, 1):
                            head_root(layer, 0)
                        if (g, c) == (6, 6):
                            act.wait_ge(ret_turned.sem, ret_turned.at(layer, 1))
                            for n in range(2):
                                ft_hi_from(PS[:, 4 + n, :].rearrange("p (h s) -> p h s", h=2), 12 + 2 * n)
                        if (g, c) == (6, 7):
                            read_natural(layer, GSV, gv, ACT.Gelu_apprx_tanh)
                        if (g, c) == (7, 0):
                            head_squares(layer, 1, gv)
                        if (g, c) == (7, 1):
                            head_root(layer, 1)
                        if (g, c) == (7, 7):
                            act.wait_ge(in_read_v.sem, in_read_v.at(layer, 3))
                            act.activation(flat(uT), flat(uT), ACT.Gelu_apprx_tanh).then_inc(u_ready.sem, 1)
                        if (g, c) == (8, 3):
                            act.wait_ge(z_step.sem, z_step.at(layer, 2))
                            for n in range(2):
                                ft_hi_from(zT[:, 2 * n:2 * n + 2, :], 4 + 2 * n)
                        if (g, c) == (8, 7):
                            read_natural(layer, GPOOL, a_nat, ACT.Copy)

                    splits(layer, g, steps, {False: in_width(g), True: in_width(g + 1)})

                def pool_steps(c):
                    if c == 0:
                        act.wait_ge(pool_psum.sem, pool_psum.at(layer, 1))
                        act.activation(flat(pT), banks(0), ACT.Copy).then_inc(pT_ready.sem, 1)
                    if c == 2:
                        act.wait_ge(poolw_psum.sem, poolw_psum.at(layer, 1))
                        for w in range(4):
                            a = act.activation(FT[:, w, 0:S], PS[:, 4 + w // 2, (w % 2) * S:(w % 2 + 1) * S], ACT.Copy,
                                               scale=pscale[:, w:w + 1])
                            if w % 2:
                                a.then_inc(ft_hi.sem, 1)

                def mlp_root(c):
                    if c == 3:
                        group_hi(layer, 0, 3, 0)
                    if c == 5:
                        root_of_mean(layer, 1, 4)

                def hi_before(f, gi, gain_row):
                    return lambda c: group_hi(layer, f, gi - 1, gain_row) if c == 3 else None

                for gi in range(4):
                    splits(layer, NIN + gi, hi_before(0, gi, 0) if gi else pool_steps)
                    evacuate_down(layer, gi, gi % 2)
                for gi in range(4):
                    splits(layer, NIN + 4 + gi, mlp_root if gi == 0 else None)
                    evacuate_up(layer, gi + 4, gi % 2, 0, gi)
                with act.Fori(0, 3) as q:
                    with act.Fori(0, 2) as i:
                        for s in range(2):
                            splits(layer, q * 8 + i * 2 + (NIN + 8 + s))
                            evacuate_down(layer, q * 8 + i * 2 + (8 + s), s)
                    with act.Fori(0, 2) as i:
                        for s in range(2):
                            splits(layer, q * 8 + i * 2 + (NIN + 12 + s))
                            evacuate_up(layer, q * 8 + i * 2 + (12 + s), s, q + 1, i * 2 + s)
                for gi in range(4):
                    splits(layer, NIN + 32 + gi, hi_before(4, gi, 1) if gi else None)
                    evacuate_down(layer, 32 + gi, gi % 2)

            last_squares(DEPTH)
            last_hi(DEPTH)
            act.wait_ge(sum_ready.sem, sum_ready.at(DEPTH, 1))
            act.activation(root[:, 0:NT], PS[:, 5, 0:NT], ACT.Sqrt, scale=1.0 / D, bias=eps).then_inc(root_ready.sem, 1)
            act.wait_ge(col_ready.sem, col_ready.at(DEPTH, 1))
            for piece in range(0, 8, 2):
                g, n = divmod(piece, NT)
                act.wait_ge(out_psum.sem, piece + 1)
                act.activation(out_sb[n][:, g * CW:(g + 1) * CW], PS[:, OUT_BANK[piece], :], ACT.Copy,
                               scale=rms_col[:, n:n + 1]).then_inc(out_s.sem, 1)

        @block.vector
        def _(dve):
            def split_lo(layer, g, k, width=CW):
                slot = k % SLOTS
                dve.wait_ge(hi_done.sem, hi_done.at(layer, g * CHUNKS + (k + 1)))
                dve.tensor_tensor(w_lo[:, slot, :, 0:width], stage[:, slot, :, 0:width],
                                  f32(w_hi[:, slot, :, 0:width]), ALU.subtract).then_inc(lo_done.sem, 1)

            def splits(layer, g, at_chunk=None, widths=None):
                for c in range(CHUNKS):
                    split_lo(layer, g, c + LEAD, (widths or {}).get(c + LEAD >= CHUNKS, CW))
                    if at_chunk:
                        at_chunk(c)

            def evacuate_up(layer, u, parity, q, gi):
                for p in range(2):
                    b = SETS[parity][2 * p]
                    dve.wait_ge(tmp_ready.sem, tmp_ready.at(layer, u * 2 + (p + 1)))
                    dve.tensor_tensor(up[:, p, :, :], PS[:, b:b + 2, 0:S], tmp[:, p, :, :], ALU.add)\
                       .then_inc(combined.sem, 1)
                    dve.wait_ge(combined.sem, combined.at(layer, u * 2 + (p + 1)))
                    dve.scalar_tensor_tensor(up[:, p, :, :], up[:, p, :, :], 0.0, up[:, p, :, :], ALU.max, ALU.mult)\
                       .then_inc(ff_ready.sem, 1)
                for p in range(2):
                    dve.wait_ge(ft_hi.sem, ft_hi.at(layer, q * 8 + gi * 2 + (8 + p + 1)))
                    tiles = ds(gi * 4 + 2 * p, 2)
                    dve.tensor_tensor(FT[:, tiles, S:2 * S], up[:, p, :, :], f32(FT[:, tiles, 0:S]), ALU.subtract)\
                       .then_inc(ft_done.sem, 1)

            def norm_lo(g_cols, tile0):
                for t in range(2):
                    one = lambda ap: ap.rearrange("p o s -> p (o s)")
                    v = dve.scalar_tensor_tensor(one(XN[:, ds(tile0 + t, 1), S:2 * S]), one(hT[:, ds(tile0 + t, 1), :]),
                                                 g_cols[:, ds(tile0 + t, 1)], one(f32(XN[:, ds(tile0 + t, 1), 0:S])),
                                                 ALU.mult, ALU.subtract)
                v.then_inc(xn_done.sem, 1)

            def evacuate_down(layer, u, parity, f, gi, last=False):
                if last:
                    dve.wait_ge(h_done.sem, h_done.at(layer, 38))
                for p in range(2):
                    b = SETS[parity][2 * p]
                    dve.wait_ge(tmp_ready.sem, tmp_ready.at(layer, u * 2 + (p + 1)))
                    dve.wait_ge(h_done.sem, h_done.at(layer, f * 8 + gi * 2 + (p - 1)))
                    dve.tensor_tensor(down[:, p, :, :], PS[:, b:b + 2, 0:S], tmp[:, p, :, :], ALU.add)\
                       .then_inc(combined.sem, 1)
                    if last:
                        dve.wait_ge(combined.sem, combined.at(layer, u * 2 + (p + 1)))
                        dve.tensor_tensor(down[:, p, :, :], down[:, p, :, :],
                                          rms2[:, :].unsqueeze(1).to_broadcast([P, 2, S]), ALU.mult).then_inc(res_step.sem, 1)
                        dve.wait_ge(res_step.sem, res_step.at(layer, p + 1))
                        tiles = slice(12 + 2 * p, 14 + 2 * p)
                        dve.tensor_tensor(hT[:, tiles, :], hT[:, tiles, :], down[:, p, :, :], ALU.add).then_inc(h_done.sem, 1)

            def group_lo(layer, norm_at, gi, gain_row, pairs=range(2)):
                for p in pairs:
                    dve.wait_ge(xn_hi.sem, xn_hi.at(layer, gi * 2 + (norm_at + p + 1)))
                    dve.wait_ge(h_done.sem, h_done.at(layer, {0: -8, 8: 0, 16: 32}[norm_at] + gi * 2 + (p + 1)))
                    norm_lo(gain[:, gain_row, :], gi * 4 + 2 * p)

            def newton(layer, m, total, mean, root, rms, rms2):
                k = [7 * m]

                def after():
                    k[0] += 1
                    return rms_step.at(layer, k[0])
                dve.wait_ge(root_ready.sem, root_ready.at(layer, m + 1))
                dve.tensor_scalar(mean, total, 1.0 / D, EPS, ALU.mult, ALU.add).then_inc(rms_step.sem, 1)
                after()
                dve.reciprocal(rms, root).then_inc(rms_step.sem, 1)
                dve.wait_ge(rms_step.sem, after())
                dve.tensor_tensor(root, rms, rms, ALU.mult).then_inc(rms_step.sem, 1)
                dve.wait_ge(rms_step.sem, after())
                dve.tensor_tensor(root, root, mean, ALU.mult).then_inc(rms_step.sem, 1)
                dve.wait_ge(rms_step.sem, after())
                dve.tensor_scalar(root, root, -0.5, 1.5, ALU.mult, ALU.add).then_inc(rms_step.sem, 1)
                dve.wait_ge(rms_step.sem, after())
                dve.tensor_tensor(rms, rms, root, ALU.mult).then_inc(rms_step.sem, 1)
                dve.wait_ge(rms_step.sem, after())
                if rms2 is not None:
                    dve.tensor_tensor(rms2, rms, rms, ALU.mult).then_inc(rms_step.sem, 1)

            def inverse_rms(layer, m, bank):
                newton(layer, m, PS[:, bank, 0:S], mean, root, rms[:, :], rms2[:, :])

            def rms_columns(layer, bank):
                dve.wait_ge(rms_turned.sem, rms_turned.at(layer, 1))
                dve.tensor_copy(rms_col[:, :], PS[:, bank, 0:NT]).then_inc(col_ready.sem, 1)

            wide_rms = rms[:, :].unsqueeze(1).to_broadcast([P, 4, S])
            heads = lambda ap: ap.rearrange("p (a n) -> p a n", a=NT * NH)

            def spread(col, n=NT * NH, width=P):
                return col.unsqueeze(2).to_broadcast([P, n, width])

            def centre(layer, k, src, dst):
                n = [10 * k]

                def after():
                    n[0] += 1
                    return norm_step.at(layer, n[0])
                dve.tensor_reduce(hn[:, 0, :], src, AX.X, ALU.add).then_inc(norm_step.sem, 1)
                dve.wait_ge(norm_step.sem, after())
                dve.tensor_scalar(hn[:, 2, :], hn[:, 0, :], 1.0 / HD, None, ALU.mult).then_inc(norm_step.sem, 1)
                dve.wait_ge(norm_step.sem, after())
                dve.tensor_tensor(dst, src, spread(hn[:, 2, :]), ALU.subtract).then_inc(norm_step.sem, 1)

            def normalise(layer, k, dst):
                n = [10 * k + 3]

                def after():
                    n[0] += 1
                    return norm_step.at(layer, n[0])
                dve.wait_ge(norm_sq.sem, norm_sq.at(layer, k + 1))
                dve.tensor_reduce(hn[:, 0, :], heads(sq_head), AX.X, ALU.add).then_inc(norm_step.sem, 1)
                dve.wait_ge(norm_step.sem, after())
                dve.tensor_scalar(hn[:, 2, :], hn[:, 0, :], 1.0 / HD, EPS, ALU.mult, ALU.add).then_inc(norm_step.sem, 1)
                after()
                dve.wait_ge(norm_root.sem, norm_root.at(layer, k + 1))
                dve.reciprocal(hn[:, 1, :], hn[:, 1, :]).then_inc(norm_step.sem, 1)
                dve.wait_ge(norm_step.sem, after())
                dve.tensor_tensor(hn[:, 3, :], hn[:, 1, :], hn[:, 1, :], ALU.mult).then_inc(norm_step.sem, 1)
                dve.wait_ge(norm_step.sem, after())
                dve.tensor_tensor(hn[:, 3, :], hn[:, 3, :], hn[:, 2, :], ALU.mult).then_inc(norm_step.sem, 1)
                dve.wait_ge(norm_step.sem, after())
                dve.scalar_tensor_tensor(hn[:, 3, :], hn[:, 3, :], 3.0, hn[:, 1, :], ALU.subtract, ALU.mult)\
                   .then_inc(norm_step.sem, 1)
                dve.wait_ge(norm_step.sem, after())
                dve.scalar_tensor_tensor(dst, dst, -0.5, spread(hn[:, 3, :]), ALU.mult, ALU.mult)\
                   .then_inc(norm_step.sem, 1)

            def ft_lo(layer, k, src, tile0):
                dve.wait_ge(ft_hi.sem, ft_hi.at(layer, k))
                dve.tensor_tensor(FT[:, tile0:tile0 + 2, S:2 * S], src, f32(FT[:, tile0:tile0 + 2, 0:S]), ALU.subtract)\
                   .then_inc(ft_done.sem, 1)

            dve.sem_inc(lo_done.sem, SLOTS)
            dve.sem_inc(chunk_used.sem, SLOTS)
            dve.sem_inc(combined.sem, 4)
            dve.sem_inc(h_done.sem, 2)
            dve.wait_ge(gain0_in.sem, 16)
            for i in range(KT // 2):
                dve.wait_ge(xT_psum.sem, i + 1)
                dve.tensor_copy(flat(hT[:, 2 * i:2 * i + 2, :]), PS[:, XT_BANK[i], :]).then_inc(hT_first.sem, 1)
                if 1 <= i <= 6:
                    dve.wait_ge(xn_hi.sem, i)
                    dve.wait_ge(hT_first.sem, i)
                    norm_lo(gain[:, 1, :], 2 * i - 2)
                if i in (3, 5, 6):
                    split_lo(0, 0, (3, 5, 6).index(i))
            dve.wait_ge(hT_first.sem, KT // 2)

            with dve.Fori(0, DEPTH) as layer:
                for g in range(NIN):
                    def steps(c):
                        if (g, c) == (0, 3):
                            group_lo(layer, 0, 3, 1)
                        if (g, c) == (0, 6):
                            inverse_rms(layer, 0, 4)
                        if (g, c) == (1, 1):
                            rms_columns(layer, 5)
                        if (g, c) == (0, 7):
                            dve.wait_ge(chunk_used.sem, group_done(layer, GQ))
                            dve.scalar_tensor_tensor(qT, banks(IN_BANK[GQ]).rearrange("p (h s) -> p h s", h=NH), Q_SCALE,
                                                     wide_rms, ALU.mult, ALU.mult).then_inc(in_read_v.sem, 1)
                        if (g, c) == (1, 7):
                            dve.wait_ge(chunk_used.sem, group_done(layer, GK))
                            dve.tensor_tensor(kT, banks(IN_BANK[GK]).rearrange("p (h s) -> p h s", h=NH), wide_rms,
                                              ALU.mult).then_inc(in_read_v.sem, 1)
                        if (g, c) == (2, 7):
                            dve.wait_ge(tab_in.sem, 16 * len(TAB_PIECES))
                            dve.wait_ge(chunk_used.sem, group_done(layer, GROT))
                            dve.wait_ge(small.sem, small.at(layer, 16 * 8))
                            dve.wait_ge(col_ready.sem, col_ready.at(layer, 1))
                            for n in range(NT):
                                dve.scalar_tensor_tensor(f_min[:, n, :], PS[:, 6 + n, 0:NH], rms_col[:, n:n + 1],
                                                         fox_bias[:, :], ALU.mult, ALU.add).then_inc(gate_z.sem, 1)
                            dve.wait_ge(gate_z.sem, gate_z.at(layer, 2))
                            dve.scalar_tensor_tensor(f_abs[:, :, :], f_min[:, :, :], -1.0, f_min[:, :, :], ALU.mult, ALU.max)\
                               .then_inc(gate_z.sem, 1)
                            dve.wait_ge(gate_z.sem, gate_z.at(layer, 3))
                            dve.tensor_scalar(f_min[:, :, :], f_min[:, :, :], 0.0, None, ALU.min).then_inc(gate_z.sem, 1)
                        if (g, c) == (3, 0):
                            dve.wait_ge(gate_z.sem, gate_z.at(layer, 4))
                            dve.wait_ge(gate_e.sem, gate_e.at(layer, 2))
                            dve.tensor_tensor(forget[:, :, :], f_min[:, :, :], f_abs[:, :, :], ALU.subtract)\
                               .then_inc(forget_ready.sem, 1)
                        if (g, c) == (3, 1):
                            dve.wait_ge(forget_ready.sem, forget_ready.at(layer, 1))
                            dve.wait_ge(forget_hi.sem, forget_hi.at(layer, 1))
                            dve.tensor_tensor(forget_b[1], spread(flat(forget[:, :, :])), f32(forget_b[0]), ALU.subtract)\
                               .then_inc(forget_ready.sem, 1)
                        if (g, c) == (3, 3):
                            dve.wait_ge(cum_psum.sem, cum_psum.at(layer, 1))
                            dve.tensor_copy(flat(cum_q[:, :, :]), PS[:, 7, 0:NT * NH]).then_inc(cum_ready.sem, 1)
                        if (g, c) in ((4, 0), (4, 1)):
                            i = c
                            if i == 0:
                                dve.wait_ge(cum_ready.sem, cum_ready.at(layer, 1))
                            dve.wait_ge(score_psum.sem, score_psum.at(layer, i + 1))
                            width = (i + 1) * P
                            for h in range(NH):
                                src = PS[:, 5, h * P:(h + 1) * P] if i == 0 else PS[:, 6 + h // 2, (h % 2) * S:(h % 2 + 1) * S]
                                dve.scalar_tensor_tensor(probs[i][:, h, :], src, cum_q[:, i, h:h + 1], mask[:, S - width:S],
                                                         ALU.add, ALU.add).then_inc(score_ready.sem, 1)
                            cols = slice(i * NH, (i + 1) * NH)
                            dve.wait_ge(score_ready.sem, score_ready.at(layer, NH * (i + 1)))
                            dve.tensor_reduce(smax[:, cols], probs[i], AX.X, ALU.max).then_inc(max_step.sem, 1)
                            dve.wait_ge(max_step.sem, max_step.at(layer, 2 * i + 1))
                            dve.tensor_scalar(smax[:, cols], smax[:, cols], -1.0, None, ALU.mult).then_inc(max_step.sem, 1)
                        if (g, c) in ((4, 2), (4, 3)):
                            i = c - 2
                            cols = slice(i * NH, (i + 1) * NH)
                            dve.wait_ge(exp_ready.sem, exp_ready.at(layer, NH * (i + 1)))
                            dve.reciprocal(ssum[:, cols], ssum[:, cols]).then_inc(recip_ready.sem, 1)
                            dve.wait_ge(recip_ready.sem, recip_ready.at(layer, i + 1))
                            dve.tensor_tensor(probs[i], probs[i], spread(ssum[:, cols], NH, (i + 1) * P), ALU.mult)\
                               .then_inc(probs_ready.sem, 1)
                        if (g, c) == (5, 0):
                            for n in range(2):
                                ft_lo(layer, n + 1, PS[:, 5 + n, :].rearrange("p (h s) -> p h s", h=2), 8 + 2 * n)
                        if (g, c) == (5, 3):
                            dve.wait_ge(ret_psum.sem, ret_psum.at(layer, 1))
                            for n, bank in enumerate((4, 7)):
                                dve.tensor_tensor(ret_s[0][:, 2 * n:2 * n + 2, :],
                                                  PS[:, bank, :].rearrange("p (h l) -> p h l", h=2),
                                                  decay[:, 2 * n:2 * n + 2, :], ALU.mult).then_inc(ret_decayed.sem, 1)
                            dve.tensor_tensor(ret_s[1], PS[:, 5, :].rearrange("p (h l) -> p h l", h=NH), decay[:, :, 0:P],
                                              ALU.mult).then_inc(ret_decayed.sem, 1)
                        if (g, c) == (5, 7):
                            dve.wait_ge(y_psum.sem, y_psum.at(layer, 1))
                            centre(layer, 0, heads(banks(6)), heads(A5[:, 0:1024]))
                        if (g, c) == (6, 1):
                            normalise(layer, 0, heads(A5[:, 0:1024]))
                        if (g, c) == (6, 6):
                            for n in range(2):
                                dve.wait_ge(ret_turned.sem, ret_turned.at(layer, 1))
                                ft_lo(layer, n + 3, PS[:, 4 + n, :].rearrange("p (h s) -> p h s", h=2), 12 + 2 * n)
                        if (g, c) == (6, 7):
                            dve.wait_ge(in_read_s.sem, in_read_s.at(layer, 10))
                            centre(layer, 1, heads(A1[:, 0:1024]), heads(A1[:, 0:1024]))
                        if (g, c) == (7, 1):
                            normalise(layer, 1, heads(A1[:, 0:1024]))
                        if (g, c) == (7, 3):
                            dve.wait_ge(ws_turned.sem, ws_turned.at(layer, 1))
                            dve.tensor_tensor(wsT[:, :, :], PS[:, 4, :].rearrange("p (h t) -> p h t", h=NH),
                                              tri.unsqueeze(1).to_broadcast([P, NH, P]), ALU.mult).then_inc(ws_ready.sem, 1)
                        if (g, c) == (7, 7):
                            dve.wait_ge(chunk_used.sem, group_done(layer, GSU))
                            dve.tensor_tensor(uT, banks(IN_BANK[GSU]).rearrange("p (h s) -> p h s", h=NH), wide_rms,
                                              ALU.mult).then_inc(in_read_v.sem, 1)
                        if (g, c) == (8, 3):
                            dve.wait_ge(z_psum.sem, z_psum.at(layer, 1))
                            dve.tensor_tensor(zT.rearrange("p h (n t) -> p h n t", n=NT),
                                              banks(6).rearrange("p (h n t) -> p h n t", h=NH, n=NT),
                                              sbias[:, :, :].unsqueeze(2).to_broadcast([P, NH, NT, P]), ALU.add)\
                               .then_inc(z_step.sem, 1)
                            dve.wait_ge(z_step.sem, z_step.at(layer, 1))
                            dve.wait_ge(u_ready.sem, u_ready.at(layer, 1))
                            dve.tensor_tensor(flat(zT), flat(zT), flat(uT), ALU.mult).then_inc(z_step.sem, 1)
                            dve.wait_ge(z_step.sem, z_step.at(layer, 2))
                            for n in range(2):
                                ft_lo(layer, n + 5, zT[:, 2 * n:2 * n + 2, :], 4 + 2 * n)

                    splits(layer, g, steps, {False: in_width(g), True: in_width(g + 1)})

                def pool_steps(c):
                    if c == 2:
                        for w in range(4):
                            if w % 2 == 0:
                                dve.wait_ge(ft_hi.sem, ft_hi.at(layer, 7 + w // 2))
                            v = dve.scalar_tensor_tensor(FT[:, w, S:2 * S], PS[:, 4 + w // 2, (w % 2) * S:(w % 2 + 1) * S],
                                                         pscale[:, w:w + 1], f32(FT[:, w, 0:S]), ALU.mult, ALU.subtract)
                            if w % 2:
                                v.then_inc(ft_done.sem, 1)

                def mlp_rms(c):
                    if c == 3:
                        group_lo(layer, 8, 3, 0)
                    if c == 5:
                        inverse_rms(layer, 1, 4)

                def lo_before(norm_at, gi, gain_row):
                    return lambda c: group_lo(layer, norm_at, gi - 1, gain_row) if c == 3 else None

                for gi in range(4):
                    splits(layer, NIN + gi, lo_before(8, gi, 0) if gi else pool_steps)
                    evacuate_down(layer, gi, gi % 2, 0, gi)
                for gi in range(4):
                    splits(layer, NIN + 4 + gi, mlp_rms if gi == 0 else None)
                    evacuate_up(layer, gi + 4, gi % 2, 0, gi)
                with dve.Fori(0, 3) as q:
                    with dve.Fori(0, 2) as i:
                        for s in range(2):
                            splits(layer, q * 8 + i * 2 + (NIN + 8 + s))
                            evacuate_down(layer, q * 8 + i * 2 + (8 + s), s, q + 1, i * 2 + s)
                    with dve.Fori(0, 2) as i:
                        for s in range(2):
                            splits(layer, q * 8 + i * 2 + (NIN + 12 + s))
                            evacuate_up(layer, q * 8 + i * 2 + (12 + s), s, q + 1, i * 2 + s)
                for gi in range(4):
                    splits(layer, NIN + 32 + gi, lo_before(16, gi, 1) if gi else None)
                    evacuate_down(layer, 32 + gi, gi % 2, 4, gi, last=gi == 3)

            group_lo(DEPTH, 0, 3, 1, pairs=(0,))
            newton(DEPTH, 0, PS[:, 5, 0:NT], mean[:, 0:NT], root[:, 0:NT], rms_col[:, :], None)
            dve.sem_inc(col_ready.sem, 1)
            group_lo(DEPTH, 0, 3, 1, pairs=(1,))
            for piece in range(1, 8, 2):
                g, n = divmod(piece, NT)
                dve.wait_ge(out_psum.sem, piece + 1)
                dve.tensor_scalar(out_sb[n][:, g * CW:(g + 1) * CW], PS[:, OUT_BANK[piece], :],
                                  rms_col[:, n:n + 1], None, ALU.mult).then_inc(out_v.sem, 1)

        @block.gpsimd
        def _(pool):
            SQ_AT = (0, 12, 12 + 16)

            def squares(layer, m, pair, first, tiles):
                if first:
                    pool.tensor_tensor(sq_acc[:, :, :], hT[:, tiles, :], hT[:, tiles, :], ALU.mult).then_inc(sq_step.sem, 2)
                else:
                    pool.tensor_tensor(sq[:, :, :], hT[:, tiles, :], hT[:, tiles, :], ALU.mult).then_inc(sq_step.sem, 1)
                    pool.wait_ge(sq_step.sem, sq_step.at(layer, pair * 2 + (SQ_AT[m] + 1)))
                    pool.tensor_tensor(sq_acc[:, :, :], sq_acc[:, :, :], sq[:, :, :], ALU.add).then_inc(sq_step.sem, 1)
                pool.wait_ge(sq_step.sem, sq_step.at(layer, pair * 2 + (SQ_AT[m] + 2)))

            def residual(layer, u, f, gi, q=None, norm=None, first=False):
                for p in range(2):
                    pool.wait_ge(combined.sem, combined.at(layer, u * 2 + (p + 1)))
                    tiles = ds(gi * 4 + 2 * p, 2)
                    if q is not None:
                        pool.wait_ge(rms_step.sem, rms_step.at(layer, 14))
                        pool.tensor_tensor(down[:, p, :, :], down[:, p, :, :],
                                           rms2[:, :].unsqueeze(1).to_broadcast([P, 2, S]), ALU.mult).then_inc(scaled.sem, 1)
                        pool.wait_ge(scaled.sem, scaled.at(layer, q * 8 + gi * 2 + (p + 1)))
                    pool.tensor_tensor(hT[:, tiles, :], hT[:, tiles, :], down[:, p, :, :], ALU.add).then_inc(h_done.sem, 1)
                if norm is not None:
                    for p in range(2):
                        pool.wait_ge(h_done.sem, h_done.at(layer, f * 8 + gi * 2 + (p + 1)))
                        squares(layer, norm, gi * 2 + p, first and p == 0, ds(gi * 4 + 2 * p, 2))

            for i in range(6):
                pool.wait_ge(hT_first.sem, i + 1)
                squares(0, 0, i, i == 0, slice(2 * i, 2 * i + 2))

            for n, (start, end) in enumerate(TAB_PIECES):
                pool.wait_ge(chunk_used.sem, SLOTS + n + 1)
                pool.dma_start(tab[:, start:end], tables[:, start:end]).then_inc(tab_in.sem, 16)

            def add_halves():
                pool.tensor_tensor(sq_acc[:, 0, :], sq_acc[:, 0, :], sq_acc[:, 1, :], ALU.add).then_inc(sq_sum.sem, 1)

            with pool.Fori(0, DEPTH) as layer:
                for p in range(2):
                    pool.wait_ge(sq_last_ready.sem, sq_last_ready.at(layer, p + 1))
                    pool.tensor_tensor(sq_acc[:, :, :], sq_acc[:, :, :], sq_last[:, 2 * p:2 * p + 2, :], ALU.add)\
                        .then_inc(sq_sum.sem, 1)
                    pool.wait_ge(sq_sum.sem, sq_sum.at(layer, p + 1))
                add_halves()
                pool.wait_ge(tab_in.sem, 16 * len(TAB_PIECES))
                pool.wait_ge(in_read_s.sem, in_read_s.at(layer, 2))
                x4 = qk.rearrange("p t (h e d) -> p t h e d", h=2 * NH, e=2)
                r4 = rot.rearrange("p t (h e d) -> p t h e d", h=2 * NH, e=2)
                t4 = rot_tmp.rearrange("p (t h d) -> p t h d", t=NT, h=2 * NH)
                cos, sin = rot_table(T_COS), rot_table(T_SIN)
                for e, (one, two, op) in enumerate(((cos, sin, ALU.subtract), (sin, cos, ALU.add))):
                    if e:
                        pool.wait_ge(rot_step.sem, rot_step.at(layer, 3))
                    pool.tensor_tensor(r4[:, :, :, e, :], x4[:, :, :, 0, :], one, ALU.mult).then_inc(rot_step.sem, 1)
                    pool.tensor_tensor(t4, x4[:, :, :, 1, :], two, ALU.mult).then_inc(rot_step.sem, 1)
                    pool.wait_ge(rot_step.sem, rot_step.at(layer, 3 * e + 2))
                    pool.tensor_tensor(r4[:, :, :, e, :], r4[:, :, :, e, :], t4, op).then_inc(rot_step.sem, 1)
                pool.wait_ge(in_read_s.sem, in_read_s.at(layer, 8))
                pool.wait_ge(small.sem, small.at(layer, 16 * 8))
                wide = lambda g: g[:, :].unsqueeze(1).to_broadcast([P, NT, GW])
                pool.tensor_tensor(swish, swish, wide(rgain), ALU.mult).then_inc(swish_gain.sem, 1)
                pool.wait_ge(swish_gain.sem, swish_gain.at(layer, 1))
                pool.wait_ge(norm_step.sem, norm_step.at(layer, 10))
                pool.tensor_tensor(y_ret, y_ret, swish, ALU.mult).then_inc(ret_out.sem, 1)
                pool.wait_ge(norm_step.sem, norm_step.at(layer, 20))
                pool.tensor_tensor(gv, gv, wide(sgain), ALU.mult).then_inc(sv_ready.sem, 1)

                for gi in range(4):
                    residual(layer, gi, 0, gi, norm=1, first=gi == 0)
                add_halves()
                with pool.Fori(0, 3) as q:
                    with pool.Fori(0, 4) as gi:
                        residual(layer, q * 8 + gi + 8, q + 1, gi, q=q)
                for gi in range(3):
                    residual(layer, 32 + gi, 4, gi, q=3, norm=2, first=gi == 0)
                pool.sem_inc(sq_ready.sem, 1)


def kernel(x, norm_mix_g, w_in, fox_b_f, pool_w, pool_scale, sgu_norm_g, sgu_w_s, sgu_b, ret_norm_g,
           w_out, norm_mlp_g, w_ff1, w_ff2, norm_final_g):
    import concourse.bacc as bacc
    from concourse.bass_utils import run_bass_kernel_spmd

    col = lambda g: np.asarray(g).reshape(KT, P).T
    after = [norm_mix_g[n] for n in range(1, DEPTH)] + [norm_final_g]
    arrays = {
        "x": np.asarray(x).reshape(S, D),
        "w_in": w_in, "w_out": w_out, "w_ff1": w_ff1, "w_ff2": w_ff2,
        "tables": constants(),
        "gain0": col(norm_mix_g[0]),
        "gains": np.stack([np.stack([col(norm_mlp_g[n]), col(after[n])], 1) for n in range(DEPTH)]),
        "fox_b": fox_b_f,
        "pool_w": np.asarray(pool_w).transpose(0, 2, 1, 3),
        "pool_scale": np.asarray(pool_scale).reshape(DEPTH, 4, P).transpose(0, 2, 1),
        "sgu_g": sgu_norm_g,
        "sgu_w": np.asarray(sgu_w_s).transpose(0, 2, 1, 3),
        "sgu_b": np.asarray(sgu_b).reshape(DEPTH, GW),
        "ret_g": ret_norm_g,
    }
    nc = bacc.Bacc("TRN2", target_bir_lowering=False, num_devices=1)
    ins, args = {}, []
    for name, a in arrays.items():
        a = np.ascontiguousarray(a)
        ins[f"in_{name}"] = a
        args.append(nc.dram_tensor(f"in_{name}", a.shape, mybir.dt.from_np(a.dtype), kind="ExternalInput").ap())
    args.append(nc.dram_tensor("out_h", (S, D), mybir.dt.float32, kind="ExternalOutput").ap())
    trunk(nc, *args)
    r = run_bass_kernel_spmd(nc, [ins], core_ids=[0])
    return r.results[0]["out_h"].reshape(1, S, D)
```
